# Optimizing a Trainium2 kernel written in Bass

```python
import jax, jax.numpy as jnp
from jax import lax
import numpy as np

D_MODEL = 1024
BATCH = 1
SEQ = 1024
DEPTH = 1

MIX_WIDTH = D_MODEL
POOL_CH = D_MODEL // 4
POOL_GROUPS = 4
POOL_GROUP_DIM = POOL_CH // POOL_GROUPS
POOL_WINDOWS = (2, 4, 8, 16)
CONV_CH = D_MODEL // 4
DW_CONV_LEN = 31
MEM_TOKENS = 256
MEM_HEADS = 4
MEM_CH = D_MODEL // 2
MEM_HEAD_DIM = MEM_CH // MEM_HEADS
IN_PROJ_WIDTH = POOL_CH + 2 * CONV_CH + MEM_CH
N_EXPERTS = 64
TOP_K = 8
EXPERT_DIM = D_MODEL // 4
SHARED_DIM = D_MODEL // 4
ROUTED_SCALE = 2.5
MOE_BLOCK = 128
LN_EPS = 1e-5
DEEPNORM_ALPHA = float((2 * DEPTH) ** 0.25)
DEEPNORM_BETA = float((8 * DEPTH) ** -0.25)

kernel_name = "hymba_pool_conformer_memattn_moe_deepnorm"

def layer_norm(x, g, b):
    xf = x.astype(jnp.float32)
    mu = jnp.mean(xf, axis=-1, keepdims=True)
    var = jnp.mean(jnp.square(xf - mu), axis=-1, keepdims=True)
    y = (xf - mu) * lax.rsqrt(var + LN_EPS) * g.astype(jnp.float32) + b.astype(jnp.float32)
    return y.astype(x.dtype)

def pool_mixer(u, w_pool, pool_scale):
    bsz, seq, _ = u.shape
    uf = u.astype(jnp.float32)
    csum = jnp.concatenate([jnp.zeros_like(uf[:, :1]), jnp.cumsum(uf, axis=1)], axis=1)
    t = jnp.arange(seq)
    pooled = []
    for g, w in enumerate(POOL_WINDOWS):
        lo = w // 2
        hi = w - 1 - lo
        start = jnp.clip(t - lo, 0, seq)
        end = jnp.clip(t + hi + 1, 0, seq)
        cs = csum[:, :, g * POOL_GROUP_DIM:(g + 1) * POOL_GROUP_DIM]
        win_sum = jnp.take(cs, end, axis=1) - jnp.take(cs, start, axis=1)
        cnt = (end - start).astype(jnp.float32)[None, :, None]
        pooled.append(win_sum / cnt)
    pooled = jnp.stack(pooled, axis=2)
    diff = pooled - uf.reshape(bsz, seq, POOL_GROUPS, POOL_GROUP_DIM)
    mixed = jnp.einsum('bsgc,gcd->bsgd', diff, w_pool.astype(jnp.float32))
    out = mixed.reshape(bsz, seq, POOL_CH) * pool_scale.astype(jnp.float32)
    return out.astype(u.dtype)

def conv_mixer(v, w_dw, b_dw, g_cn, b_cn):
    a, gate = jnp.split(v, 2, axis=-1)
    glu = a * jax.nn.sigmoid(gate)
    pad = DW_CONV_LEN // 2
    y = lax.conv_general_dilated(
        glu, w_dw[:, None, :].astype(glu.dtype), window_strides=(1,), padding=[(pad, pad)],
        dimension_numbers=('NWC', 'WIO', 'NWC'), feature_group_count=CONV_CH) + b_dw
    return jax.nn.silu(layer_norm(y, g_cn, b_cn))

def mem_attention(q, mem_n, w_kv):
    bsz, seq, _ = q.shape
    kv = mem_n @ w_kv
    k, v = jnp.split(kv, 2, axis=-1)
    q = q.reshape(bsz, seq, MEM_HEADS, MEM_HEAD_DIM)
    k = k.reshape(bsz, -1, MEM_HEADS, MEM_HEAD_DIM)
    v = v.reshape(bsz, -1, MEM_HEADS, MEM_HEAD_DIM)
    s = jnp.einsum('bshd,bmhd->bhsm', q, k).astype(jnp.float32) * (MEM_HEAD_DIM ** -0.5)
    p = jax.nn.softmax(s, axis=-1).astype(v.dtype)
    o = jnp.einsum('bhsm,bmhd->bshd', p, v)
    return o.reshape(bsz, seq, MEM_CH)

def swiglu(x, wg, wu, wd):
    return (jax.nn.silu(x @ wg) * (x @ wu)) @ wd

def moe(x, w_router, router_bias, w_gate, w_up, w_down, w_gate_sh, w_up_sh, w_down_sh):
    bsz, seq, d = x.shape
    n_tok = bsz * seq
    xt = x.reshape(n_tok, d)
    scores = jax.nn.sigmoid((xt @ w_router).astype(jnp.float32))
    _, idx = lax.top_k(scores + router_bias.astype(jnp.float32), TOP_K)
    sel = jnp.take_along_axis(scores, idx, axis=-1)
    gates = sel / jnp.sum(sel, axis=-1, keepdims=True) * ROUTED_SCALE

    n_assign = n_tok * TOP_K
    e_flat = idx.reshape(-1)
    tok_flat = jnp.arange(n_assign, dtype=jnp.int32) // TOP_K
    gate_flat = gates.reshape(-1)
    order = jnp.argsort(e_flat)
    e_sorted = e_flat[order]
    counts = jnp.bincount(e_flat, length=N_EXPERTS)
    starts = jnp.cumsum(counts) - counts
    padded = (counts + MOE_BLOCK - 1) // MOE_BLOCK * MOE_BLOCK
    padded_end = jnp.cumsum(padded)
    padded_start = padded_end - padded
    dest = padded_start[e_sorted] + jnp.arange(n_assign, dtype=jnp.int32) - starts[e_sorted]
    n_blocks = -(-n_assign // MOE_BLOCK) + N_EXPERTS
    buf_len = n_blocks * MOE_BLOCK
    tok_buf = jnp.full((buf_len,), n_tok, jnp.int32).at[dest].set(tok_flat[order])
    gate_buf = jnp.zeros((buf_len,), jnp.float32).at[dest].set(gate_flat[order])
    block_expert = jnp.minimum(
        jnp.searchsorted(padded_end, jnp.arange(n_blocks) * MOE_BLOCK, side='right'), N_EXPERTS - 1)
    x_pad = jnp.concatenate([xt, jnp.zeros((1, d), xt.dtype)], axis=0)

    def expert_block(acc, blk):
        tok, g, e = blk
        xb = x_pad[tok]
        h = jax.nn.silu(xb @ w_gate[e]) * (xb @ w_up[e])
        y = (h @ w_down[e]) * g[:, None].astype(xb.dtype)
        return acc.at[tok].add(y), None

    routed, _ = lax.scan(
        expert_block, jnp.zeros_like(x_pad),
        (tok_buf.reshape(n_blocks, MOE_BLOCK), gate_buf.reshape(n_blocks, MOE_BLOCK), block_expert))
    shared = swiglu(xt, w_gate_sh, w_up_sh, w_down_sh)
    return (routed[:n_tok] + shared).reshape(bsz, seq, d)

def setup_inputs(seed: int = 0) -> dict:
    key = jax.random.key(seed)
    ks = jax.random.split(key, 26)
    f32 = jnp.float32
    nrm = lambda k, shape, scale: jax.random.normal(k, shape, f32) * scale
    L = DEPTH
    return {
        "x": nrm(ks[0], (BATCH, SEQ, D_MODEL), 1.0),
        "mem": nrm(ks[1], (BATCH, MEM_TOKENS, D_MODEL), 1.0),
        "w_in": nrm(ks[2], (L, D_MODEL, IN_PROJ_WIDTH), D_MODEL ** -0.5),
        "w_pool": nrm(ks[3], (L, POOL_GROUPS, POOL_GROUP_DIM, POOL_GROUP_DIM), POOL_GROUP_DIM ** -0.5),
        "pool_scale": 1.0 + nrm(ks[4], (L, POOL_CH), 0.02),
        "w_dw": nrm(ks[5], (L, DW_CONV_LEN, CONV_CH), DW_CONV_LEN ** -0.5),
        "b_dw": nrm(ks[6], (L, CONV_CH), 0.02),
        "conv_norm_g": 1.0 + nrm(ks[7], (L, CONV_CH), 0.02),
        "conv_norm_b": nrm(ks[8], (L, CONV_CH), 0.02),
        "w_kv": nrm(ks[9], (L, D_MODEL, 2 * MEM_CH), D_MODEL ** -0.5),
        "w_out": nrm(ks[10], (L, MIX_WIDTH, D_MODEL), MIX_WIDTH ** -0.5 * DEEPNORM_BETA),
        "ln1_g": 1.0 + nrm(ks[11], (L, D_MODEL), 0.02),
        "ln1_b": nrm(ks[12], (L, D_MODEL), 0.02),
        "w_router": nrm(ks[13], (L, D_MODEL, N_EXPERTS), D_MODEL ** -0.5),
        "router_bias": nrm(ks[14], (L, N_EXPERTS), 0.01),
        "w_gate": nrm(ks[15], (L, N_EXPERTS, D_MODEL, EXPERT_DIM), D_MODEL ** -0.5),
        "w_up": nrm(ks[16], (L, N_EXPERTS, D_MODEL, EXPERT_DIM), D_MODEL ** -0.5),
        "w_down": nrm(ks[17], (L, N_EXPERTS, EXPERT_DIM, D_MODEL), EXPERT_DIM ** -0.5 * DEEPNORM_BETA),
        "w_gate_sh": nrm(ks[18], (L, D_MODEL, SHARED_DIM), D_MODEL ** -0.5),
        "w_up_sh": nrm(ks[19], (L, D_MODEL, SHARED_DIM), D_MODEL ** -0.5),
        "w_down_sh": nrm(ks[20], (L, SHARED_DIM, D_MODEL), SHARED_DIM ** -0.5 * DEEPNORM_BETA),
        "ln2_g": 1.0 + nrm(ks[21], (L, D_MODEL), 0.02),
        "ln2_b": nrm(ks[22], (L, D_MODEL), 0.02),
        "mem_norm_g": 1.0 + nrm(ks[23], (D_MODEL,), 0.02),
        "mem_norm_b": nrm(ks[24], (D_MODEL,), 0.02),
    }

def reference(x, mem, w_in, w_pool, pool_scale, w_dw, b_dw, conv_norm_g, conv_norm_b, w_kv, w_out,
              ln1_g, ln1_b, w_router, router_bias, w_gate, w_up, w_down, w_gate_sh, w_up_sh, w_down_sh,
              ln2_g, ln2_b, mem_norm_g, mem_norm_b):
    mem_n = layer_norm(mem, mem_norm_g, mem_norm_b)
    for l in range(DEPTH):
        proj = x @ w_in[l]
        u = proj[..., :POOL_CH]
        v = proj[..., POOL_CH:POOL_CH + 2 * CONV_CH]
        q = proj[..., POOL_CH + 2 * CONV_CH:]
        y_pool = pool_mixer(u, w_pool[l], pool_scale[l])
        y_conv = conv_mixer(v, w_dw[l], b_dw[l], conv_norm_g[l], conv_norm_b[l])
        y_mem = mem_attention(q, mem_n, w_kv[l])
        mix = jnp.concatenate([y_pool, y_conv, y_mem], axis=-1) @ w_out[l]
        x = layer_norm(DEEPNORM_ALPHA * x + mix, ln1_g[l], ln1_b[l])
        ffn = moe(x, w_router[l], router_bias[l], w_gate[l], w_up[l], w_down[l],
                  w_gate_sh[l], w_up_sh[l], w_down_sh[l])
        x = layer_norm(DEEPNORM_ALPHA * x + ffn, ln2_g[l], ln2_b[l])
    return x


_drawn_inputs = setup_inputs


def setup_inputs(seed=0):
    import zlib

    import numpy as np

    out = dict(_drawn_inputs(seed))
    spreads = {}
    factors = {'pool_scale': 10.256,
     'b_dw': 3.132,
     'conv_norm_g': 12.042,
     'conv_norm_b': 11.91,
     'ln2_g': 20.662,
     'ln2_b': 21.341,
     'mem_norm_g': 8.0,
     'mem_norm_b': 10.68}
    for name, (base, spread) in spreads.items():
        noise = np.random.default_rng([zlib.crc32(name.encode()), seed]).standard_normal(out[name].shape)
        drawn = base * np.exp(spread * noise) if base else spread * noise
        out[name] = __import__('jax').numpy.asarray(drawn.astype(out[name].dtype))
    for name, factor in factors.items():
        out[name] = (out[name] * factor).astype(out[name].dtype)
    return out
```

```python
import concourse.bass as bass
from concourse import mybir
from contextlib import ExitStack

F = mybir.dt.float32
R = mybir.dt.float32r
BF = mybir.dt.bfloat16
I32 = mybir.dt.int32
U32 = mybir.dt.uint32
ALU = mybir.AluOpType
ACT = mybir.ActivationFunctionType
AX = mybir.AxisListType

S = 1024
D = 1024
NT = S // 128
ND = D // 128
POOL_WINDOWS = (2, 4, 8, 16)
TAPS = 31
PAD = TAPS // 2
M = 256
HEADS = 4
DH = 128
E = 64
K = 8
XD = 256
NE = E + 1
MAX_ITEMS = NT + E + (S * K - E) // 128
STEPS = 137
LIST = NE * S + 128 * 160
EPS = 1e-5
ALPHA = float(2 ** 0.25)
SCALE = float(DH) ** -0.5
ROUTED = 2.5
PRODS = ((0, 0), (0, 1), (1, 0))
KB = 1024


def build(nc, a, out, only_x1=False):
    ctx = ExitStack()
    base = 16512

    def at(name, kb, shape, dt=F):
        return nc.alloc_sbuf_tensor_at(name, shape, dt, offset=base + int(kb * KB))

    def sem(name):
        return ctx.enter_context(nc.semaphore(name))

    with ctx:
        xT = at("xT", 0, [128, 2, ND, S], R)
        wo = at("wo", 0, [128, 2, 8, D], R)
        wgu = at("wgu", 0, [128, 2, 2, ND, 512], R)
        wdn = at("wdn", 64, [128, 2, 2, 2, D], R)
        qT = at("qT", 64, [128, HEADS, S])
        memin = at("memin", 64, [128, 2, D])
        mixA = at("mixA", 80, [128, 4, S])
        memT = at("memT", 80, [128, 2, ND, M], R)
        kT = at("kT", 96, [128, 2, HEADS, M], R)
        vv = at("vv", 104, [128, 2, 2, 512], R)
        xTe = at("xTe", 96, [128, 2, 2, ND, 128], R)
        raw = at("raw", 112, [128, 2, 3, 2048])
        wraw = at("wraw", 112, [128, 3, ND, 128])
        xin = at("xin", 124, [128, 3, D])
        whl = at("whl", 136, [128, 2, 2, ND, 128], R)
        uP = at("uP", 152, [128, 2, S + 16])
        glu = at("glu", 160.25, [128, 2, S + 32])
        cv = at("cv", 168.5, [128, 2, S])
        buf1 = at("buf1", 176.5, [128, 2, S + 16])
        buf2 = at("buf2", 184.75, [128, 2, S + 16])
        diff = at("diff", 193, [128, 2, S])
        mtmp = at("mtmp", 124, [128, ND, M])
        zero = at("zero", 201, [128, 512])
        mst = at("mst", 136, [128, 2, 8, 128], R)
        qst = at("qst", 144, [128, 2, 2, HEADS, 128], R)
        x1T = at("x1T", 152, [128, 2, ND, 128], R)
        xres = at("xres", 160, [128, 2, D])
        g1 = at("g1", 168, [128, D])
        b1 = at("b1", 172, [128, D])
        wrr = at("wrr", 201, [128, ND, E])
        wrt = at("wrt", 176, [128, 2, ND, E], R)
        pr = at("pr", 180, [128, HEADS, M])
        pT = at("pT", 184, [128, 2, 8, 128], R)
        oh = at("oh", 192, [128, K, E])
        ohx = at("ohx", 194, [128, K, E])
        sc = at("sc", 196, [128, E])
        sb_ = at("sb_", 196.25, [128, E])
        rankS = at("rankS", 196.5, [128, E])
        rbias = at("rbias", 196.75, [128, E])
        iotaE = at("iotaE", 197, [128, E])
        maskb = at("maskb", 197.25, [128, E], BF)
        maskf = at("maskf", 197.5, [128, E])
        cumb = at("cumb", 197.75, [128, 2, E], BF)
        cumf = at("cumf", 198, [128, E])
        top8 = at("top8", 198.25, [128, 8])
        idxu = at("idxu", 198.3125, [128, 8], U32)
        sel = at("sel", 198.375, [128, 8])
        addrf = at("addrf", 198.4375, [128, 8])
        addr = at("addr", 198.5, [128, 2, 8], U32)
        xg = at("xg", 160, [128, 2, D])
        hs = at("hs", 168, [128, 2, XD])
        hx = at("hx", 170, [128, 2, XD])
        hT = at("hT", 172, [128, 2, 2, 2, 128], R)
        ysb = at("ysb", 176, [128, 2, D])
        idx = at("idx", 184, [128, 2], U32)
        cmp_ = at("cmp_", 192, [128, 2, NE])
        cmpx = at("cmpx", 193, [128, 2, NE])
        tabf = at("tabf", 194, [128, 3, 2])
        tab = at("tab", 185, [1, 3, 256], I32)
        nit = at("nit", 188.25, [1, 8], I32)
        yg = at("yg", 0, [128, 2, K, D])
        xsh = at("xsh", 64, [128, 2, D])
        x1c = at("x1c", 72, [128, 2, D])
        acc = at("acc", 80, [128, 2, D])
        g2 = at("g2", 96, [128, D])
        b2 = at("b2", 100, [128, D])
        ohc = at("ohc", 104, [128, K, E])
        ohd = at("ohd", 106, [128, K, E])
        yrow = at("yrow", 108, [128, 2, K], U32)
        iotaC = at("iotaC", 109, [128, E])
        sel2 = at("sel2", 109.5, [128, K])
        neghalf = at("neghalf", 207.6875, [128, 2])
        epst = at("epst", 207.71875, [128, 1])
        ident = at("ident", 203, [128, 128])
        tri = at("tri", 203.5, [128, 128], BF)
        oneb = at("oneb", 203.75, [128, 128], BF)
        ones = at("ones", 204, [128, 128])
        bd = at("bd", 204.5, [128, 2, 128])
        mgb = at("mgb", 205.5, [128, 2, ND])
        wdw = at("wdw", 205.5625, [128, 2, TAPS])
        cpar = at("cpar", 205.875, [128, 4, 2])
        edge = at("edge", 205.9375, [128, 2, 16])
        gates = at("gates", 206.0625, [128, NT, K])
        idxf = at("idxf", 206.3125, [128, NT, K])
        rankK = at("rankK", 206.5625, [128, NT, K])
        stat = at("stat", 206.8125, [128, 2, 2, 6])
        mv = at("mv", 206.90625, [128, 2, 2])
        sm = at("sm", 206.9375, [128, 3, HEADS])
        tok = at("tok", 207, [128, 2], U32)
        tokf = at("tokf", 207.03125, [128, 2])
        rs = at("rs", 207.0625, [128, 4])
        gs = at("gs", 207.09375, [128, 4])
        startE = at("startE", 207.125, [128, NE])
        endE = at("endE", 207.40625, [128, NE])
        fillw = at("fillw", 200.4375, [128, 96], U32)
        cnt65 = at("cnt65", 198.625, [128, NE])
        blk = at("blk", 199, [128, NE])
        blki = at("blki", 199.375, [128, NE], I32)
        itemp = at("itemp", 199.75, [128, 2])
        ones65 = at("ones65", 200, [128, NE])
        idlist = at("idlist", 200.375, [128, 8], U32)

        ps = ctx.enter_context(nc.psum_tensor("ps", [128, 8, 512], F))

        x1_d = nc.dram_tensor("x1_d", [S, D], F, kind="Internal").ap()
        list_d = nc.dram_tensor("list_d", [LIST, 1], U32, kind="Internal").ap()
        y_d = nc.dram_tensor("y_d", [(MAX_ITEMS + 1) * 128, D], F, kind="Internal").ap()

        s_const = sem("s_const")
        s_iden = sem("s_iden")
        s_par = sem("s_par")
        s_bd = sem("s_bd")
        s_x = [sem(f"s_xin{i}") for i in range(3)]
        s_mem = sem("s_mem")
        s_w = [sem(f"s_w{i}") for i in range(3)]
        s_xt = sem("s_xt")
        s_xhi = sem("s_xhi")
        s_xlo = sem("s_xlo")
        s_whi = sem("s_whi")
        s_wlo = sem("s_wlo")
        s_job = sem("s_job")
        s_gfree = [sem("s_g0"), sem("s_g1")]
        s_sig = sem("s_sig")
        s_glu = sem("s_glu")
        s_u = sem("s_u")
        s_pool = sem("s_pool")
        s_diff = sem("s_diff")
        s_mln = sem("s_mln")
        s_mt = sem("s_mt")
        s_mtc = sem("s_mtc")
        s_mhi = sem("s_mhi")
        s_mlo = sem("s_mlo")
        s_kvhi = sem("s_kvhi")
        s_v = sem("s_v")
        s_a = sem("s_a")
        s_yc = sem("s_yc")
        s_sq = sem("s_sq")
        s_yn = sem("s_yn")
        s_mix = sem("s_mix")
        s_endP = sem("s_endP")

        W_JOBS = ["gate0", "a0", "gate1", "a1", "u0", "u1", "K0", "K1", "K2", "K3",
                  "V0", "V1", "V2", "V3", "q0", "q1", "q2", "q3"]
        JOBS = W_JOBS[:15] + ["pool0", "pool1"] + W_JOBS[15:] + ["mean", "var"]
        WCOL = {"gate0": 4, "a0": 2, "gate1": 5, "a1": 3, "u0": 0, "u1": 1,
                "q0": 6, "q1": 7, "q2": 8, "q3": 9}
        TAPS_IN = {"u0": 10, "u1": 10, "q0": 9, "q1": 9, "q2": 9, "q3": 7}
        TAPS_IN.update({w: 1 for w in W_JOBS[6:14]})
        taps = [(k, c) for k in range(TAPS) for c in range(2)]

        def w_src(n):
            w = W_JOBS[n]
            if w in WCOL:
                return a["w_in"][WCOL[w]]
            return a["w_kv"][int(w[1]) + (4 if w[0] == "V" else 0)]

        def result(j):
            return 4 + 2 * (j % 2)

        def wait_result_free(eng, j):
            if j >= 2:
                eng.wait_ge(s_gfree[j % 2], j // 2)

        block = ctx.enter_context(nc.Block())

        T = {}

        for n_ in ("s_wo s_wol s_wohi s_wolo s_t0 s_xr0 s_xr1 s_gb s_wrhi s_wr s_st s_stl s_S s_negm s_max s_exp s_rden s_p s_pt "
                   "s_pthi s_ptlo s_ot s_ohi s_olo s_pre s_var s_mr s_hat s_x1 s_x1w0 s_x1w1 s_tr s_x1hi s_x1lo s_lg "
                   "s_scr s_mask s_rk s_rkc s_addr s_sc0 s_sc1 s_fill s_endT s_vt s_at s_pt2 s_lgf").split():
            T[n_] = sem(n_)
        (s_wo, s_wol, s_wohi, s_wolo, s_t0, s_xr0, s_xr1, s_gb, s_wrhi, s_wr, s_st, s_stl, s_S, s_negm, s_max, s_exp, s_rden, s_p,
         s_pt, s_pthi, s_ptlo, s_ot, s_ohi, s_olo, s_pre, s_var, s_mr, s_hat, s_x1, s_x1w0, s_x1w1, s_tr, s_x1hi, s_x1lo,
         s_lg, s_scr, s_mask, s_rk, s_rkc, s_addr, s_sc0, s_sc1, s_fill, s_endT, s_vt, s_at, s_pt2, s_lgf) = T.values()
        s_xr, s_x1w, s_sc = (s_xr0, s_xr1), (s_x1w0, s_x1w1), (s_sc0, s_sc1)
        s_tabs = sem("s_tabs")
        s_stm, s_pre_pe, s_wrl, s_scu, s_cumf, s_cnt = (sem(n) for n in (
            "s_stm", "s_pre_pe", "s_wrl", "s_scu", "s_cumf", "s_cnt"))
        s_seen = sem("s_seen")
        s_zero = sem("s_zero")
        s_cvd, s_ic = sem("s_cvd"), sem("s_ic")
        s_pv, s_pw, s_sd = sem("s_pv"), sem("s_pw"), sem("s_sd")
        s_cm = sem("s_cm")
        s_tabp = sem("s_tabp")
        s_rw = (sem("s_rw0"), sem("s_rw1"))
        s_ready = sem("s_ready")
        s_rfree = sem("s_rfree")
        s_ghi, s_glo, s_dhi, s_dlo = sem("s_ghi"), sem("s_glo"), sem("s_dhi"), sem("s_dlo")
        s_idx = (sem("s_idx0"), sem("s_idx1"))
        s_xg = (sem("s_xg0"), sem("s_xg1"))
        s_et, s_ehi, s_elo = sem("s_et"), sem("s_ehi"), sem("s_elo")
        s_gu, s_silu, s_h = sem("s_gu"), sem("s_silu"), sem("s_h")
        s_ht, s_hhi, s_hlo = sem("s_ht"), sem("s_hhi"), sem("s_hlo")
        s_dn, s_y = sem("s_dn"), sem("s_y")
        s_yd = (sem("s_yd0"), sem("s_yd1"))
        s_xgz = sem("s_xgz")
        s_endR = sem("s_endR")
        s_cl = (sem("s_cl0"), sem("s_cl1"))
        s_g2 = sem("s_g2")
        s_yr = sem("s_yr")
        s_yg = (sem("s_yg0"), sem("s_yg1"))
        s_vc = sem("s_vc")
        s_acc, s_nr, s_o = sem("s_acc"), sem("s_nr"), sem("s_o")
        s_out = (sem("s_out0"), sem("s_out1"))

        def seg_wait(eng, sems, value):
            for s in sems:
                eng.wait_ge(s, value)

        @block.sync
        def _(sp):
            sp.dma_start(mgb[:], a["mem_gb"]).then_inc(s_par, 16)
            sp.dma_start(wdw[:], a["w_dw"]).then_inc(s_par, 16)
            sp.dma_start(cpar[:], a["cpar"]).then_inc(s_par, 16)
            sp.dma_start(edge[:], a["edge"]).then_inc(s_par, 16)
            sp.wait_ge(s_const, 1)
            for g in range(4):
                o = 64 * (g % 2)
                sp.dma_start(bd[o:o + 64, g // 2, o:o + 64], a["w_pool"][g]).then_inc(s_bd, 16)
            for n in range(18):
                if n >= 3:
                    sp.wait_ge(s_wlo, n - 2)
                sp.dma_start(wraw[:, n % 3], w_src(n)).then_inc(s_w[n % 3], 16)
                if n == 2:
                    for m in range(2):
                        sp.dma_start(memin[:, m], a["mem"][m]).then_inc(s_mem, 16)
            sp.wait_ge(s_pool, 5)
            for n in range(NT + E, MAX_ITEMS + 1, 16):
                for h in range(2):
                    sp.dma_start(y_d[n * 128:(n + 16) * 128, h * 512:(h + 1) * 512].rearrange("(i p) d -> p i d", p=128),
                                 zero[:].unsqueeze(1).to_broadcast([128, 16, 512])).then_inc(s_zero, 16)
            sp.wait_ge(s_wlo, 18)
            for n in range(4):
                if n == 3:
                    sp.wait_ge(s_wolo, 1)
                sp.dma_start(raw[:, 0, n % 3], a["w_out"][n]).then_inc(s_w[n % 3], 16)
            sp.wait_ge(s_endP, 4)
            sp.wait_ge(s_zero, 16 * 8)
            for dst, src in ((g1, "ln1_g"), (b1, "ln1_b"), (rbias, "router_bias")):
                sp.dma_start(dst[:], a[src].to_broadcast([128, dst.shape[1]])).then_inc(s_gb, 16)
            sp.dma_start(wrr[:], a["w_router"]).then_inc(s_wr, 16)
            for t in range(2):
                sp.dma_start(xres[:, t], a["x"][t]).then_inc(s_xr[t], 16)
            sp.wait_ge(s_wolo, 4)
            for n, w in enumerate(("sh_gate", "sh_up", "sh_down")):
                sp.dma_start(raw[:, 0, n], a[w]).then_inc(s_rw[0], 16)
            for t in range(NT):
                sp.wait_ge(s_x1, t + 1)
                sp.dma_start(x1_d[t * 128:(t + 1) * 128, :], xres[:, t % 2]).then_inc(s_x1w[t % 2], 16)
                if t + 2 < NT:
                    sp.wait_ge(s_x1w[t % 2], 16 * (t // 2 + 1))
                    sp.wait_ge(s_tr, t + 1)
                    sp.dma_start(xres[:, t % 2], a["x"][t + 2]).then_inc(s_xr[t % 2], 16)
            if only_x1:
                for s in range(2):
                    sp.wait_ge(s_x1w[s], 16 * 4)
                sp.wait_ge(s_endT, 4)
                sp.dma_start(out, x1_d).then_inc(s_out[0], 16)
                sp.wait_ge(s_out[0], 16)
                return
            sp.wait_ge(s_endT, 4)
            sp.dma_start(raw[:, 1, 0], a["w_gate"][0]).then_inc(s_rw[1], 16)
            sp.dma_start(raw[:, 1, 1], a["w_up"][0]).then_inc(s_rw[1], 16)
            sp.dma_start(raw[:, 1, 2], a["w_down"][0]).then_inc(s_rw[1], 16)
            sp.wait_ge(s_rw[0], 48)
            sp.sem_inc(s_ready, 1)

            def load_expert(e, s, nth):
                sp.wait_ge(s_rfree, e - 1)
                for n, w in enumerate(("w_gate", "w_up", "w_down")):
                    sp.dma_start(raw[:, s, n], a[w][bass.ds(e - 1, 1)].rearrange("a p n -> (a p) n")
                                 ).then_inc(s_rw[s], 16)
                sp.wait_ge(s_rw[1 - s], nth)
                sp.sem_inc(s_ready, 1)

            with sp.Fori(0, 31) as jj:
                load_expert(2 * jj + 2, 0, 48 * (jj + 1))
                load_expert(2 * jj + 3, 1, 48 * (jj + 2))
            load_expert(64, 0, 48 * 32)
            sp.wait_ge(s_rw[0], 48 * 33)
            sp.sem_inc(s_ready, 1)
            sp.wait_ge(s_endR, 4)
            sp.dma_start(g2[:], a["ln2_g"].to_broadcast([128, D])).then_inc(s_g2, 16)
            sp.dma_start(b2[:], a["ln2_b"].to_broadcast([128, D])).then_inc(s_g2, 16)
            for t in range(2):
                sp.dma_start(x1c[:, t], x1_d[t * 128:(t + 1) * 128, :]).then_inc(s_cl[t], 16)
                sp.dma_start(xsh[:, t], y_d[t * 128:(t + 1) * 128, :]).then_inc(s_cl[t], 16)
            for t in range(NT):
                s = t % 2
                if t + 2 < NT:
                    sp.wait_ge(s_acc, t + 1)
                    r = slice((t + 2) * 128, (t + 3) * 128)
                    sp.dma_start(x1c[:, s], x1_d[r, :]).then_inc(s_cl[s], 16)
                    sp.dma_start(xsh[:, s], y_d[r, :]).then_inc(s_cl[s], 16)
                sp.wait_ge(s_o, t + 1)
                sp.dma_start(out[t * 128:(t + 1) * 128, :], acc[:, s]).then_inc(s_out[s], 16)
            for s in range(2):
                sp.wait_ge(s_out[s], 16 * 4)

        @block.gpsimd
        def _(g):
            g.memset(bd[:], 0.0).then_inc(s_const, 1)
            for t in range(3):
                g.dma_start(xin[:, t], a["x"][t]).then_inc(s_x[t], 16)
            g.memset(zero[:], 0.0).then_inc(s_pool, 1)
            g.memset(ident[:], 0.0).then_inc(s_pool, 1)
            g.memset(tri[:], 1.0).then_inc(s_pool, 1)
            g.memset(ones[:], 1.0 / 256).then_inc(s_const, 1)
            g.memset(oneb[:], 1.0).then_inc(s_const, 1)
            g.memset(neghalf[:], -0.5).then_inc(s_pool, 1)
            g.memset(epst[:], EPS).then_inc(s_pool, 1)
            g.wait_ge(s_pool, 5)
            g.affine_select(out=ident[:], in_=ident[:], compare_op=ALU.not_equal, fill=1.0, base=0,
                            pattern=[[-1, 128]], channel_multiplier=1).then_inc(s_iden, 1)
            g.affine_select(out=tri[:], in_=tri[:], compare_op=ALU.is_gt, fill=0.0, base=0,
                            pattern=[[1, 128]], channel_multiplier=-1).then_inc(s_const, 1)
            g.memset(uP[:, :, 0:8], 0.0).then_inc(s_const, 1)
            g.memset(uP[:, :, S + 8:S + 16], 0.0).then_inc(s_const, 1)
            g.memset(glu[:, :, 0:PAD], 0.0).then_inc(s_const, 1)
            g.memset(glu[:, :, PAD + S:S + 32], 0.0).then_inc(s_const, 1)
            for t in range(3, NT):
                g.wait_ge(s_xt, t - 2)
                g.dma_start(xin[:, t % 3], a["x"][t]).then_inc(s_x[t % 3], 16)
            g.wait_ge(s_pv, 1)
            g.tensor_tensor(mv[:, :, 1], mv[:, :, 1], neghalf[:], ALU.pow).then_inc(s_pw, 1)
            g.wait_ge(s_u, 2)
            g.wait_ge(s_const, 8)
            n = 5
            W = S + 16

            def step(ins):
                nonlocal n
                ins.then_inc(s_pool, 1)
                n += 1
                g.wait_ge(s_pool, n)
            step(g.tensor_tensor(buf1[:, :, 0:W - 1], uP[:, :, 0:W - 1], uP[:, :, 1:W], ALU.add))
            step(g.tensor_tensor(buf2[:, :, 0:W - 3], buf1[:, :, 0:W - 3], buf1[:, :, 2:W - 1], ALU.add))

            def mean_minus_token(grp, buf):
                w = POOL_WINDOWS[grp]
                p, c, lo = slice(64 * (grp % 2), 64 * (grp % 2) + 64), grp // 2, 8 - w // 2
                step(g.tensor_scalar(diff[p, c, :], buf[p, c, lo:lo + S], 1.0 / w, None, ALU.mult))
                for t0, e0 in ((0, 0), (S - 8, 8)):
                    step(g.tensor_tensor(diff[p, c, t0:t0 + 8], buf[p, c, lo + t0:lo + t0 + 8],
                                         edge[p, c, e0:e0 + 8], ALU.mult))
                step(g.tensor_tensor(diff[p, c, :], diff[p, c, :], uP[p, c, 8:8 + S], ALU.subtract))
            g.wait_ge(s_par, 64)
            mean_minus_token(0, buf1)
            mean_minus_token(1, buf2)
            step(g.tensor_tensor(buf1[:, 1, 0:W - 7], buf2[:, 1, 0:W - 7], buf2[:, 1, 4:W - 3], ALU.add))
            mean_minus_token(2, buf1)
            step(g.tensor_tensor(buf2[:, 1, 0:W - 15], buf1[:, 1, 0:W - 15], buf1[:, 1, 8:W - 7], ALU.add))
            mean_minus_token(3, buf2)
            g.sem_inc(s_diff, 1)
            g.sem_inc(s_endP, 1)
            g.wait_ge(s_endP, 4)
            g.iota(iotaE[:], pattern=[[1, E]], base=0, channel_multiplier=0,
                   allow_small_or_imprecise_dtypes=True).then_inc(s_pt2, 1)
            g.iota(tokf[:], pattern=[[128, 2]], base=0, channel_multiplier=1,
                   allow_small_or_imprecise_dtypes=True).then_inc(s_pt2, 1)
            g.iota(itemp[:], pattern=[[128, 2]], base=0, channel_multiplier=1,
                   allow_small_or_imprecise_dtypes=True).then_inc(s_pt2, 1)
            g.iota(idlist[:], pattern=[[1, 8]], base=0, channel_multiplier=8).then_inc(s_pt2, 1)
            g.iota(fillw[:], pattern=[[0, 96]], base=2048, channel_multiplier=0).then_inc(s_pt2, 1)
            g.memset(ones65[:], 1.0).then_inc(s_pt2, 1)
            g.memset(cumf[:], 0.0).then_inc(s_pt2, 1)
            g.memset(cumb[:], 0.0).then_inc(s_pt2, 1)
            g.wait_ge(s_pt2, 8)
            g.dma_start(list_d[0:S, :].rearrange("(p j) a -> p (j a)", j=8), idlist[:]).then_inc(s_fill, 16)
            for n in range(7):
                g.dma_start(list_d[S + n * 12288:S + (n + 1) * 12288, :].rearrange("(p j) a -> p (j a)", p=128),
                            fillw[:]).then_inc(s_fill, 16)
            g.wait_ge(s_fill, 128)
            def rstd(n):
                g.wait_ge(s_pv, n)
                g.tensor_tensor(rs[:, 0:1], mv[:, 0, 1:2], neghalf[:, 0:1], ALU.pow).then_inc(s_pw, 1)

            rstd(2)
            for t in range(NT):
                if t + 1 < NT:
                    rstd(t + 3)
                g.wait_ge(s_addr, t + 1)
                for k in range(K):
                    g.indirect_dma_start(
                        out=list_d, out_offset=bass.IndirectOffsetOnAxis(ap=addr[:, t % 2, k:k + 1], axis=0),
                        in_=tok[:, t % 2:t % 2 + 1], in_offset=None,
                        bounds_check=LIST - 1, oob_is_err=True).then_inc(s_sc[t % 2], 16)
            if only_x1:
                for s in range(2):
                    g.wait_ge(s_sc[s], 16 * K * 4)
                g.sem_inc(s_endT, 1)
                return
            for s in range(2):
                g.wait_ge(s_sc[s], 16 * K * 4)
            g.sem_inc(s_endT, 1)
            g.wait_ge(s_endT, 4)
            for s in range(2):
                g.wait_ge(s_x1w[s], 16 * 4)
            g.memset(xg[:], 0.0).then_inc(s_xgz, 1)
            g.wait_ge(s_xgz, 1)
            for i in range(2):
                g.dma_start(idx[:, i:i + 1], list_d[i * 128:(i + 1) * 128, :]).then_inc(s_idx[i], 16)
            g.wait_ge(s_idx[0], 16)

            def gather(s):
                g.indirect_dma_start(
                    out=xg[:, s], out_offset=None, in_=x1_d,
                    in_offset=bass.IndirectOffsetOnAxis(ap=idx[:, s:s + 1], axis=0),
                    bounds_check=S - 1, oob_is_err=False).then_inc(s_xg[s], 16)
            gather(0)
            g.wait_ge(s_tabs, 1)
            n_items = g.value_load(nit[0:1, 0:1], min_val=NT + E, max_val=MAX_ITEMS)

            def fetch(i, s, nth):
                g.wait_ge(s_idx[1 - s], 16 * nth[1 - s])
                if not isinstance(i, int) or i > 0:
                    g.wait_ge(s_et, i)
                g.sem_inc(s_seen, 1)
                gather(1 - s)
                lb = g.value_load(tab[0:1, 2, bass.ds(i + 2, 1)], min_val=0, max_val=LIST - 128)
                g.wait_ge(s_xg[s], 16 * nth[s])
                g.sem_inc(s_seen, 1)
                g.dma_start(idx[:, s:s + 1], list_d[bass.ds(lb, 128), :]).then_inc(s_idx[s], 16)

            fetch(0, 0, (1, 1))
            with g.Fori(0, (STEPS - 1) // 2) as jj:
                with g.If(n_items > 2 * jj):
                    fetch(2 * jj + 1, 1, (jj + 2, jj + 1))
                with g.If(n_items > 2 * jj + 1):
                    fetch(2 * jj + 2, 0, (jj + 2, jj + 2))
            g.wait_ge(s_et, n_items + 2)
            g.sem_inc(s_endR, 1)
            g.wait_ge(s_endR, 4)
            g.iota(iotaC[:], pattern=[[1, E]], base=0, channel_multiplier=0,
                   allow_small_or_imprecise_dtypes=True).then_inc(s_ic, 1)
            for t in range(NT):
                s = t % 2
                if t >= 2:
                    g.wait_ge(s_acc, t - 1)
                g.wait_ge(s_yr, t + 1)
                for k in range(K):
                    g.indirect_dma_start(
                        out=yg[:, s, k], out_offset=None, in_=y_d,
                        in_offset=bass.IndirectOffsetOnAxis(ap=yrow[:, s, k:k + 1], axis=0),
                        bounds_check=MAX_ITEMS * 128 - 1, oob_is_err=True).then_inc(s_yg[s], 16)
                if t >= 1:
                    rstd(NT + 1 + t)
            rstd(2 * NT + 1)
            for s in range(2):
                g.wait_ge(s_yg[s], 16 * K * 4)

        @block.scalar
        def _(act):
            def split_hi(n):
                act.wait_ge(s_w[n % 3], 16 * (n // 3 + 1))
                if n >= 2:
                    j = JOBS.index(W_JOBS[n - 2])
                    act.wait_ge(s_job, j + 1)
                nc.scalar.copy(whl[:, n % 2, 0], wraw[:, n % 3]).then_inc(s_whi, 1)

            split_hi(0)
            for t in range(NT):
                act.wait_ge(s_xt, t + 1)
                for b in range(2):
                    nc.scalar.copy(xT[:, 0, 4 * b:4 * b + 4, t * 128:(t + 1) * 128],
                                   ps[:, 2 * (t % 2) + b, :].rearrange("p (c n) -> p c n", c=4)).then_inc(s_xhi, 1)
            na = 0
            for j, w in enumerate(JOBS):
                s, b = j % 2, result(j)
                both = ps[:, b:b + 2, :].rearrange("p a n -> p (a n)")
                if w in W_JOBS and W_JOBS.index(w) < 17:
                    split_hi(W_JOBS.index(w) + 1)
                if w == "u1":
                    act.wait_ge(s_mtc, 1)
                    nc.scalar.copy(memT[:, 0, 0:4], mtmp[:, 0:4]).then_inc(s_mhi, 1)
                    nc.scalar.copy(memT[:, 0, 4:8], mtmp[:, 4:8]).then_inc(s_mhi, 1)
                if w != "mean" and w != "var":
                    act.wait_ge(s_job, j + 1)
                if w[:4] == "gate":
                    c = int(w[4])
                    nc.scalar.activation(glu[:, c, PAD:PAD + S], both, ACT.Sigmoid).then_inc(s_sig, 1)
                    act.wait_ge(s_sig, c + 1)
                    act.sem_inc(s_gfree[s], 1)
                elif w[0] == "u":
                    nc.scalar.copy(uP[:, int(w[1]), 8:8 + S], both).then_inc(s_u, 1)
                    act.wait_ge(s_u, int(w[1]) + 1)
                    act.sem_inc(s_gfree[s], 1)
                elif w[0] == "K":
                    nc.scalar.copy(kT[:, 0, int(w[1])], ps[:, b, 0:M]).then_inc(s_kvhi, 1)
                elif w[0] == "V":
                    c = int(w[1])
                    nc.scalar.copy(vv[:, 0, :, c * 128:(c + 1) * 128],
                                   ps[:, b, 0:256].rearrange("p (m n) -> p m n", m=2)).then_inc(s_kvhi, 1)
                elif w[0] == "q":
                    nc.scalar.copy(qT[:, int(w[1])], both).then_inc(s_gfree[s], 1)
                elif w[:4] == "pool":
                    c = int(w[4])
                    nc.scalar.activation(mixA[:, c], both, ACT.Copy, scale=cpar[:, 3, c:c + 1]).then_inc(s_gfree[s], 1)
                elif w == "mean":
                    act.wait_ge(s_yc, 1)
                    act.wait_ge(s_diff, 1)
                    nc.scalar.activation(buf1[:, :, 0:S], cv[:], ACT.Square).then_inc(s_sq, 1)
                elif w == "var":
                    act.wait_ge(s_job, j + 1)
                    nc.scalar.activation(buf2[:, 1, 0:S], both, ACT.Sqrt, bias=epst[:]).then_inc(s_sd, 1)
                    act.wait_ge(s_yn, 1)
                    for c in range(2):
                        nc.scalar.activation(mixA[:, 2 + c], cv[:, c], ACT.Silu, bias=cpar[:, 2, c:c + 1],
                                             scale=cpar[:, 1, c:c + 1]).then_inc(s_mix, 1)
            for n in range(4):
                act.wait_ge(s_w[n % 3], 16 * (6 + n // 3 + 1))
                if n == 0:
                    act.wait_ge(s_job, JOBS.index("q3") + 1)
                nc.scalar.copy(wo[:, 0, 2 * n:2 * n + 2],
                               raw[:, 0, n % 3].rearrange("p (c n) -> p c n", c=2)).then_inc(s_wohi, 1)
            act.wait_ge(s_mix, 2)
            act.wait_ge(s_wohi, 4)
            act.sem_inc(s_endP, 1)
            act.wait_ge(s_endP, 4)

            act.wait_ge(s_wr, 16)
            nc.scalar.copy(wrt[:, 0], wrr[:]).then_inc(s_wrhi, 1)

            def stage_q(t):
                s = t % 2
                if t >= 2:
                    act.wait_ge(s_S, t - 1)
                nc.scalar.copy(qst[:, s, 0], qT[:, :, t * 128:(t + 1) * 128]).then_inc(s_st, 1)

            def stage_mix(t):
                if t >= 1:
                    act.wait_ge(s_pre_pe, t)
                nc.scalar.copy(mst[:, 0, 0:4], mixA[:, :, t * 128:(t + 1) * 128]).then_inc(s_stm, 1)

            stage_q(0)
            for t in range(NT + 2):
                if t < NT:
                    for h in range(HEADS):
                        act.wait_ge(s_negm, 4 * t + h + 1)
                        nc.scalar.activation(pr[:, h], ps[:, h // 2, (h % 2) * M:(h % 2 + 1) * M], ACT.Exp,
                                             bias=sm[:, 0, h:h + 1], scale=SCALE,
                                             accum_out=sm[:, 1, h:h + 1]).then_inc(s_exp, 1)
                    if t + 1 < NT:
                        stage_q(t + 1)
                    for h in range(HEADS):
                        act.wait_ge(s_rden, t + 1)
                        nc.scalar.activation(pr[:, h], pr[:, h], ACT.Copy, scale=sm[:, 2, h:h + 1]).then_inc(s_p, 1)
                if 1 <= t <= NT:
                    act.wait_ge(s_mr, t)
                    nc.scalar.activation(xres[:, (t - 1) % 2], xres[:, (t - 1) % 2], ACT.Identity,
                                         bias=rs[:, 1:2], scale=rs[:, 0:1]).then_inc(s_hat, 1)
                if t < NT:
                    for b in range(2):
                        act.wait_ge(s_pt, 2 * t + b + 1)
                        nc.scalar.copy(pT[:, 0, 4 * b:4 * b + 4],
                                       ps[:, 2 + b, :].rearrange("p (c n) -> p c n", c=4)).then_inc(s_pthi, 1)
                    stage_mix(t)
                    act.wait_ge(s_ot, t + 1)
                    nc.scalar.copy(mst[:, 0, 4:8], ps[:, 4, :].rearrange("p (c n) -> p c n", c=4)).then_inc(s_ohi, 1)
                if 1 <= t <= NT:
                    act.wait_ge(s_tr, t)
                    for b in range(2):
                        nc.scalar.copy(x1T[:, 0, 4 * b:4 * b + 4],
                                       ps[:, 2 + b, :].rearrange("p (c n) -> p c n", c=4)).then_inc(s_x1hi, 1)
                    act.wait_ge(s_lg, t)
                    nc.scalar.activation(sc[:], ps[:, 7, 0:E], ACT.Sigmoid).then_inc(s_scr, 1)
            act.wait_ge(s_scr, NT)
            act.sem_inc(s_endT, 1)
            if only_x1:
                return
            act.wait_ge(s_endT, 4)
            act.wait_ge(s_ready, 1)

            def split_gu_hi(slot, rslot):
                for n in range(2):
                    nc.scalar.copy(wgu[:, slot, 0, :, n * XD:(n + 1) * XD],
                                   raw[:, rslot, n].rearrange("p (c n) -> p c n", c=ND)).then_inc(s_ghi, 1)

            def split_dn_hi(slot, rslot):
                nc.scalar.copy(wdn[:, slot, 0], raw[:, rslot, 2].rearrange("p (c n) -> p c n", c=2)).then_inc(s_dhi, 1)

            def item_hi(i, s, slot_free):
                act.wait_ge(s_et, i + 1)
                if slot_free is not None:
                    act.wait_ge(s_gu, slot_free)
                for b in range(2):
                    nc.scalar.copy(xTe[:, s, 0, 4 * b:4 * b + 4],
                                   ps[:, b, :].rearrange("p (c n) -> p c n", c=4)).then_inc(s_ehi, 1)

            split_gu_hi(0, 0)
            item_hi(0, 0, None)
            split_dn_hi(0, 0)
            act.wait_ge(s_tabs, 1)
            n_items = act.value_load(nit[0:1, 0:1], min_val=NT + E, max_val=MAX_ITEMS)

            def step_act(i, s, jj):
                first = isinstance(i, int)
                nxt = 1 if first else act.value_load(tab[0:1, 1, bass.ds(i, 1)], min_val=0, max_val=E)
                item_hi(i + 1, 1 - s, None if first else i)

                def gu():
                    act.wait_ge(s_ready, nxt + 1)
                    slot = nxt % 2
                    v = bass.ds(slot, 1)
                    for n in range(2):
                        nc.scalar.copy(wgu[:, v, 0, :, n * XD:(n + 1) * XD].rearrange("p a c n -> p (a c) n"),
                                       raw[:, v, n].rearrange("p a (c n) -> p (a c) n", c=ND)).then_inc(s_ghi, 1)

                def dn():
                    v = bass.ds(nxt % 2, 1)
                    nc.scalar.copy(wdn[:, v, 0].rearrange("p a c n -> p (a c) n"),
                                   raw[:, v, 2].rearrange("p a (c n) -> p (a c) n", c=2)).then_inc(s_dhi, 1)
                if first:
                    gu()
                else:
                    with act.If(nxt > 0):
                        gu()
                act.wait_ge(s_gu, i + 1)
                nc.scalar.activation(hs[:, s], ps[:, 2 + s, 0:XD], ACT.Silu).then_inc(s_silu, 1)
                if not first:
                    with act.If(jj > 0):
                        act.wait_ge(s_yd[1 - s], 16 * jj)
                        act.sem_inc(s_seen, 1)
                    act.wait_ge(s_dn, i)
                    for b in range(2):
                        nc.scalar.copy(ysb[:, 1 - s, b * 512:(b + 1) * 512], ps[:, 5 + b, :]).then_inc(s_y, 1)
                act.wait_ge(s_ht, i + 1)
                nc.scalar.copy(hT[:, s, 0], ps[:, 4, 0:256].rearrange("p (c n) -> p c n", c=2)).then_inc(s_hhi, 1)
                if not first:
                    act.wait_ge(s_y, 2 * i)
                    act.dma_start(y_d[bass.ds((i - 1) * 128, 128), :], ysb[:, 1 - s]).then_inc(s_yd[1 - s], 16)
                if first:
                    dn()
                else:
                    with act.If(nxt > 0):
                        dn()

            step_act(0, 0, 0)
            with act.Fori(0, (STEPS - 1) // 2) as jj:
                with act.If(n_items > 2 * jj):
                    step_act(2 * jj + 1, 1, jj)
                with act.If(n_items > 2 * jj + 1):
                    step_act(2 * jj + 2, 0, jj)
            act.wait_ge(s_yd[0], 16 * ((n_items + 1) // 2))
            act.wait_ge(s_yd[1], 16 * (n_items // 2))
            act.wait_ge(s_hhi, n_items + 1)
            act.sem_inc(s_endR, 1)
            act.wait_ge(s_endR, 4)
            for t in range(NT):
                act.wait_ge(s_nr, t + 1)
                nc.scalar.activation(acc[:, t % 2], acc[:, t % 2], ACT.Identity,
                                     bias=rs[:, 1:2], scale=rs[:, 0:1]).then_inc(s_hat, 1)


        @block.vector
        def _(v):
            nv = 0
            V = nc.vector

            def step(ins):
                nonlocal nv
                ins.then_inc(s_v, 1)
                nv += 1

            def settle():
                v.wait_ge(s_v, nv)

            def split_lo(n):
                v.wait_ge(s_whi, n + 1)
                V.tensor_tensor(whl[:, n % 2, 1], wraw[:, n % 3], whl[:, n % 2, 0].bitcast(F),
                                ALU.subtract).then_inc(s_wlo, 1)

            split_lo(0)
            for t in range(NT):
                for b in range(2):
                    v.wait_ge(s_xhi, 2 * t + b + 1)
                    cols = slice(t * 128, (t + 1) * 128)
                    last = V.tensor_tensor(xT[:, 1, 4 * b:4 * b + 4, cols],
                                           ps[:, 2 * (t % 2) + b, :].rearrange("p (c n) -> p c n", c=4),
                                           xT[:, 0, 4 * b:4 * b + 4, cols].bitcast(F), ALU.subtract)
                last.then_inc(s_xlo, 1)
            v.wait_ge(s_mem, 32)
            for m in range(2):
                for b in range(2):
                    step(V.bn_stats(stat[:, m, b], memin[:, m, b * 512:(b + 1) * 512]))
            settle()
            for m in range(2):
                step(V.bn_aggr(mv[:, m], stat[:, m].rearrange("p a b -> p (a b)")))
            settle()
            V.tensor_scalar(mv[:, :, 1], mv[:, :, 1], EPS, None, ALU.add).then_inc(s_pv, 1)
            v.wait_ge(s_pw, 1)
            for m in range(2):
                V.tensor_scalar(memin[:, m], memin[:, m], mv[:, m, 0:1], mv[:, m, 1:2], ALU.subtract,
                                ALU.mult).then_inc(s_mln, 1)
            kvhi = tap = 0
            for j, w in enumerate(JOBS):
                s, b = j % 2, result(j)
                both = ps[:, b:b + 2, :].rearrange("p a n -> p (a n)")
                if w in W_JOBS and W_JOBS.index(w) < 17:
                    split_lo(W_JOBS.index(w) + 1)
                for _ in range(TAPS_IN.get(w, 0)):
                    k, c = taps[tap]
                    if k == 0:
                        v.wait_ge(s_par, 64)
                        v.wait_ge(s_const, 8)
                        if c == 0:
                            v.wait_ge(s_glu, 2)
                        step(V.tensor_scalar(cv[:, c], glu[:, c, 0:S], wdw[:, c, 0:1], cpar[:, 0, c:c + 1],
                                             ALU.mult, ALU.add))
                    else:
                        v.wait_ge(s_v, nv - 1)
                        step(V.scalar_tensor_tensor(cv[:, c], glu[:, c, k:k + S], wdw[:, c, k:k + 1], cv[:, c],
                                                    ALU.mult, ALU.add))
                    tap += 1
                if w == "a1":
                    for m in range(2):
                        v.wait_ge(s_mt, m + 1)
                        for c in range(ND):
                            step(V.tensor_scalar(mtmp[:, c, m * 128:(m + 1) * 128],
                                                 ps[:, 2 * m + c // 4, (c % 4) * 128:(c % 4 + 1) * 128],
                                                 mgb[:, 0, c:c + 1], mgb[:, 1, c:c + 1], ALU.mult, ALU.add))
                    settle()
                    v.sem_inc(s_mtc, 1)
                if w == "u1":
                    for b_ in range(2):
                        v.wait_ge(s_mhi, b_ + 1)
                        V.tensor_tensor(memT[:, 1, 4 * b_:4 * b_ + 4], mtmp[:, 4 * b_:4 * b_ + 4],
                                        memT[:, 0, 4 * b_:4 * b_ + 4].bitcast(F), ALU.subtract).then_inc(s_mlo, 1)
                if w[0] == "a":
                    c = int(w[1])
                    v.wait_ge(s_job, j + 1)
                    v.wait_ge(s_sig, c + 1)
                    V.tensor_tensor(glu[:, c, PAD:PAD + S], both, glu[:, c, PAD:PAD + S], ALU.mult).then_inc(s_glu, 1)
                    v.wait_ge(s_glu, c + 1)
                    v.sem_inc(s_gfree[s], 1)
                elif w[0] == "K":
                    kvhi += 1
                    v.wait_ge(s_kvhi, kvhi)
                    V.tensor_tensor(kT[:, 1, int(w[1])], ps[:, b, 0:M], kT[:, 0, int(w[1])].bitcast(F),
                                    ALU.subtract).then_inc(s_gfree[s], 1)
                elif w[0] == "V":
                    kvhi += 1
                    c = slice(int(w[1]) * 128, int(w[1]) * 128 + 128)
                    v.wait_ge(s_kvhi, kvhi)
                    V.tensor_tensor(vv[:, 1, :, c], ps[:, b, 0:256].rearrange("p (m n) -> p m n", m=2),
                                    vv[:, 0, :, c].bitcast(F), ALU.subtract).then_inc(s_gfree[s], 1)
                elif w == "mean":
                    v.wait_ge(s_job, j + 1)
                    for c in range(2):
                        step(V.tensor_tensor(cv[:, c], cv[:, c], both, ALU.subtract))
                    settle()
                    v.sem_inc(s_yc, 1)
                    v.sem_inc(s_gfree[s], 1)
                elif w == "var":
                    v.wait_ge(s_job, j + 1)
                    v.wait_ge(s_sd, 1)
                    step(V.reciprocal(buf2[:, 0, 0:S], buf2[:, 1, 0:S]))
                    settle()
                    for c in range(2):
                        step(V.tensor_tensor(cv[:, c], cv[:, c], buf2[:, 0, 0:S], ALU.mult))
                    settle()
                    v.sem_inc(s_yn, 1)
                if w == "q2":
                    pass
                if w == "q3":
                    settle()
                    v.sem_inc(s_cvd, 1)
            assert tap == len(taps)
            for n in range(4):
                v.wait_ge(s_wohi, n + 1)
                V.tensor_tensor(wo[:, 1, 2 * n:2 * n + 2], raw[:, 0, n % 3].rearrange("p (c n) -> p c n", c=2),
                                wo[:, 0, 2 * n:2 * n + 2].bitcast(F), ALU.subtract).then_inc(s_wolo, 1)
            v.wait_ge(s_wolo, 4)
            v.sem_inc(s_endP, 1)
            v.wait_ge(s_endP, 4)

            v.wait_ge(s_wrhi, 1)
            V.tensor_tensor(wrt[:, 1], wrr[:], wrt[:, 0].bitcast(F), ALU.subtract).then_inc(s_wrl, 1)
            v.wait_ge(s_gb, 48)
            v.wait_ge(s_pt2, 8)

            def stage_q(t):
                v.wait_ge(s_st, t + 1)
                V.tensor_tensor(qst[:, t % 2, 1], qT[:, :, t * 128:(t + 1) * 128],
                                qst[:, t % 2, 0].bitcast(F), ALU.subtract).then_inc(s_stl, 1)

            stage_q(0)
            for t in range(NT + 2):
                if t < NT:
                    v.wait_ge(s_S, t + 1)
                    for hh in range(2):
                        step(V.tensor_reduce(sm[:, 0, 2 * hh:2 * hh + 2],
                                             ps[:, hh, :].rearrange("p (h n) -> p h n", h=2), AX.X, ALU.max))
                    settle()
                    V.tensor_scalar(sm[:, 0], sm[:, 0], -SCALE, None, ALU.mult).then_inc(s_negm, 4)
                    if t + 1 < NT:
                        stage_q(t + 1)
                    v.wait_ge(s_exp, 4 * t + 4)
                    V.reciprocal(sm[:, 2], sm[:, 1]).then_inc(s_rden, 1)
                if 1 <= t <= NT:
                    r = (t - 1) % 2
                    v.wait_ge(s_pre_pe, t)
                    v.wait_ge(s_xr[r], 16 * ((t - 1) // 2 + 1))
                    for b in range(2):
                        step(V.scalar_tensor_tensor(xres[:, r, b * 512:(b + 1) * 512],
                                                    xres[:, r, b * 512:(b + 1) * 512], ALPHA, ps[:, 5 + b, :],
                                                    ALU.mult, ALU.add))
                    settle()
                    v.sem_inc(s_pre, 1)
                    for b in range(2):
                        step(V.bn_stats(stat[:, 0, b], xres[:, r, b * 512:(b + 1) * 512]))
                    settle()
                    step(V.bn_aggr(mv[:, 0], stat[:, 0].rearrange("p a b -> p (a b)")))
                    settle()
                    V.tensor_scalar(mv[:, 0, 1:2], mv[:, 0, 1:2], EPS, None, ALU.add).then_inc(s_pv, 1)
                    v.wait_ge(s_pw, 1 + t)
                    V.scalar_tensor_tensor(rs[:, 1:2], mv[:, 0, 0:1], -1.0, rs[:, 0:1], ALU.mult,
                                           ALU.mult).then_inc(s_mr, 1)
                    v.wait_ge(s_hat, t)
                    step(V.tensor_tensor(xres[:, r], xres[:, r], g1[:], ALU.mult))
                    settle()
                    V.tensor_tensor(xres[:, r], xres[:, r], b1[:], ALU.add).then_inc(s_x1, 1)
                if t < NT:
                    for b in range(2):
                        v.wait_ge(s_pthi, 2 * t + b + 1)
                        V.tensor_tensor(pT[:, 1, 4 * b:4 * b + 4],
                                        ps[:, 2 + b, :].rearrange("p (c n) -> p c n", c=4),
                                        pT[:, 0, 4 * b:4 * b + 4].bitcast(F), ALU.subtract).then_inc(s_ptlo, 1)
                    v.wait_ge(s_stm, t + 1)
                    V.tensor_tensor(mst[:, 1, 0:4], mixA[:, :, t * 128:(t + 1) * 128], mst[:, 0, 0:4].bitcast(F),
                                    ALU.subtract).then_inc(s_olo, 1)
                    v.wait_ge(s_ohi, t + 1)
                    V.tensor_tensor(mst[:, 1, 4:8], ps[:, 4, :].rearrange("p (c n) -> p c n", c=4),
                                    mst[:, 0, 4:8].bitcast(F), ALU.subtract).then_inc(s_olo, 1)
                if t >= 2:
                    u = t - 2
                    v.wait_ge(s_rk, u + 1)
                    step(V.tensor_copy(rankS[:], ps[:, 7, 128:128 + E]))
                    settle()
                    v.sem_inc(s_rkc, 1)
                    step(V.tensor_tensor(ohx[:], oh[:], rankS[:].unsqueeze(1).to_broadcast([128, K, E]), ALU.mult))
                    settle()
                    step(V.tensor_reduce(rankK[:, u], ohx[:], AX.X, ALU.add))
                    settle()
                    step(V.scalar_tensor_tensor(addrf[:], idxf[:, u], float(S), rankK[:, u], ALU.mult, ALU.add))
                    settle()
                    if u >= 2:
                        v.wait_ge(s_sc[u % 2], 16 * K * (u // 2))
                    step(V.tensor_scalar(addr[:, u % 2], addrf[:], float(S), None, ALU.add))
                    step(V.tensor_scalar(tok[:, u % 2:u % 2 + 1], tokf[:, 0:1], float(128 * u), None, ALU.add))
                    settle()
                    v.sem_inc(s_addr, 1)
                if 1 <= t <= NT:
                    u = t - 1
                    for b in range(2):
                        v.wait_ge(s_x1hi, 2 * u + b + 1)
                        V.tensor_tensor(x1T[:, 1, 4 * b:4 * b + 4],
                                        ps[:, 2 + b, :].rearrange("p (c n) -> p c n", c=4),
                                        x1T[:, 0, 4 * b:4 * b + 4].bitcast(F), ALU.subtract).then_inc(s_x1lo, 1)
                    v.wait_ge(s_scr, u + 1)
                    step(V.tensor_tensor(sb_[:], sc[:], rbias[:], ALU.add))
                    settle()
                    step(V.max(top8[:], sb_[:]))
                    settle()
                    step(V.max_index(idxu[:], top8[:], sb_[:]))
                    settle()
                    step(V.tensor_copy(idxf[:, u], idxu[:]))
                    settle()
                    step(V.tensor_tensor(oh[:], iotaE[:].unsqueeze(1).to_broadcast([128, K, E]),
                                         idxf[:, u].unsqueeze(2).to_broadcast([128, K, E]), ALU.is_equal))
                    settle()
                    step(V.tensor_reduce(maskf[:], oh[:].rearrange("p k e -> p e k"), AX.X, ALU.add))
                    settle()
                    step(V.tensor_copy(maskb[:], maskf[:]))
                    if u >= 1:
                        pass
                    settle()
                    v.sem_inc(s_mask, 1)
                    step(V.tensor_tensor(ohx[:], oh[:], sc[:].unsqueeze(1).to_broadcast([128, K, E]), ALU.mult))
                    step(V.tensor_tensor(cumf[:], cumf[:], maskf[:], ALU.add))
                    settle()
                    v.sem_inc(s_scu, 1)
                    step(V.tensor_copy(cumb[:, (u + 1) % 2], cumf[:]))
                    step(V.tensor_reduce(sel[:], ohx[:], AX.X, ALU.add))
                    settle()
                    step(V.tensor_reduce(gs[:, 0:1], sel[:], AX.X, ALU.add))
                    settle()
                    step(V.reciprocal(gs[:, 1:2], gs[:, 0:1]))
                    settle()
                    step(V.tensor_scalar(gates[:, u], sel[:], gs[:, 1:2], ROUTED, ALU.mult, ALU.mult))
            settle()
            v.sem_inc(s_cumf, 1)
            v.wait_ge(s_cnt, 1)
            step(V.tensor_copy(cnt65[:, 1:NE], ps[:, 7, 128:128 + E]))
            step(V.memset(cnt65[:, 0:1], float(S)))
            settle()
            step(V.tensor_scalar(blki[:], cnt65[:], 127.0, None, ALU.add))
            settle()
            step(V.tensor_scalar(blki[:], blki[:], 7, None, ALU.arith_shift_right))
            settle()
            step(V.tensor_copy(blk[:], blki[:]))
            settle()
            step(V.tensor_scalar(blk[:], blk[:], 1.0, None, ALU.max))
            settle()
            step(V.tensor_tensor_scan(endE[:], ones65[:], blk[:], 0.0, ALU.mult, ALU.add))
            settle()
            step(V.tensor_tensor(startE[:], endE[:], blk[:], ALU.subtract))
            for b in range(2):
                step(V.tensor_scalar(cmp_[:, b], endE[:], itemp[:, b:b + 1], None, ALU.is_le))
            settle()
            for b in range(2):
                step(V.tensor_tensor(cmpx[:, b], cmp_[:, b], blk[:], ALU.mult))
            settle()
            step(V.tensor_reduce(tabf[:, 0], cmp_[:], AX.X, ALU.add))
            step(V.tensor_reduce(tabf[:, 1], cmpx[:], AX.X, ALU.add))
            settle()
            step(V.tensor_tensor(tabf[:, 2], itemp[:], tabf[:, 1], ALU.subtract))
            settle()
            step(V.tensor_scalar(tabf[:, 1], tabf[:, 2], 0.0, None, ALU.is_equal))
            step(V.tensor_scalar(tabf[:, 2], tabf[:, 2], 128.0, None, ALU.mult))
            settle()
            step(V.scalar_tensor_tensor(tabf[:, 2], tabf[:, 0], float(S), tabf[:, 2], ALU.mult, ALU.add))
            step(V.tensor_scalar(cmp_[:, :, 0], tabf[:, 0], float(E), None, ALU.is_lt))
            step(V.tensor_scalar(cmp_[:, :, 1], tabf[:, 0], 1.0, None, ALU.add))
            settle()
            step(V.tensor_tensor(tabf[:, 1], tabf[:, 1], cmp_[:, :, 0], ALU.mult))
            settle()
            step(V.tensor_tensor(tabf[:, 1], tabf[:, 1], cmp_[:, :, 1], ALU.mult))
            step(V.tensor_scalar(tabf[:, 0], tabf[:, 0], float(E), None, ALU.min))
            settle()
            v.sem_inc(s_cm, 1)
            v.sem_inc(s_endT, 1)
            if only_x1:
                return
            v.wait_ge(s_endT, 4)
            v.wait_ge(s_tabp, 1)
            step(V.tensor_copy(tab[:].rearrange("p a b -> p (a b)"),
                               ps[0:1, 4:6, :].rearrange("p a n -> p (a n)")[:, 0:768]))
            step(V.tensor_copy(nit[0:1, 0:1], endE[0:1, NE - 1:NE]))
            settle()
            v.sem_inc(s_tabs, 1)
            n_items = v.value_load(nit[0:1, 0:1], min_val=NT + E, max_val=MAX_ITEMS)

            def lo(dst, raw_, hi, done):
                V.tensor_tensor(dst, raw_, hi.bitcast(F), ALU.subtract).then_inc(done, 1)

            def item_lo(i, s):
                for b in range(2):
                    v.wait_ge(s_ehi, 2 * i + b + 1)
                    last = V.tensor_tensor(xTe[:, s, 1, 4 * b:4 * b + 4],
                                           ps[:, b, :].rearrange("p (c n) -> p c n", c=4),
                                           xTe[:, s, 0, 4 * b:4 * b + 4].bitcast(F), ALU.subtract)
                last.then_inc(s_elo, 1)

            def split_lo_gu(e):
                w = bass.ds(e % 2, 1)
                for n in range(2):
                    v.wait_ge(s_ghi, 2 * e + n + 1)
                    cols = slice(n * XD, (n + 1) * XD)
                    lo(wgu[:, w, 1, :, cols].rearrange("p a c n -> p (a c) n"),
                       raw[:, w, n].rearrange("p a (c n) -> p (a c) n", c=ND),
                       wgu[:, w, 0, :, cols].rearrange("p a c n -> p (a c) n"), s_glo)

            def split_lo_dn(e):
                w = bass.ds(e % 2, 1)
                v.wait_ge(s_dhi, e + 1)
                lo(wdn[:, w, 1].rearrange("p a c n -> p (a c) n"),
                   raw[:, w, 2].rearrange("p a (c n) -> p (a c) n", c=2),
                   wdn[:, w, 0].rearrange("p a c n -> p (a c) n"), s_dlo)
                v.wait_ge(s_dlo, e + 1)
                v.wait_ge(s_glo, 2 * e + 2)
                v.sem_inc(s_rfree, 1)

            split_lo_gu(0)
            item_lo(0, 0)
            split_lo_dn(0)

            def step_v(i, s):
                first = isinstance(i, int)
                nxt = 1 if first else v.value_load(tab[0:1, 1, bass.ds(i, 1)], min_val=0, max_val=E)
                item_lo(i + 1, 1 - s)
                if first:
                    split_lo_gu(1)
                else:
                    with v.If(nxt > 0):
                        split_lo_gu(nxt)
                v.wait_ge(s_silu, i + 1)
                V.tensor_tensor(hx[:, s], hs[:, s], ps[:, 2 + s, XD:2 * XD], ALU.mult).then_inc(s_h, 1)
                v.wait_ge(s_hhi, i + 1)
                V.tensor_tensor(hT[:, s, 1], ps[:, 4, 0:256].rearrange("p (c n) -> p c n", c=2),
                                hT[:, s, 0].bitcast(F), ALU.subtract).then_inc(s_hlo, 1)
                if first:
                    split_lo_dn(1)
                else:
                    with v.If(nxt > 0):
                        split_lo_dn(nxt)

            step_v(0, 0)
            with v.Fori(0, (STEPS - 1) // 2) as jj:
                with v.If(n_items > 2 * jj):
                    step_v(2 * jj + 1, 1)
                with v.If(n_items > 2 * jj + 1):
                    step_v(2 * jj + 2, 0)
            v.wait_ge(s_hlo, n_items + 1)
            v.sem_inc(s_endR, 1)
            v.wait_ge(s_endR, 4)
            step(V.tensor_scalar(startE[:], startE[:], 128.0, None, ALU.mult))
            settle()

            def rows(t):
                if t >= 2:
                    v.wait_ge(s_yg[t % 2], 16 * K * (t // 2))
                step(V.tensor_tensor(ohc[:], iotaC[:].unsqueeze(1).to_broadcast([128, K, E]),
                                     idxf[:, t].unsqueeze(2).to_broadcast([128, K, E]), ALU.is_equal))
                settle()
                step(V.tensor_tensor(ohd[:], ohc[:], startE[:, 1:NE].unsqueeze(1).to_broadcast([128, K, E]), ALU.mult))
                settle()
                step(V.tensor_reduce(sel2[:], ohd[:], AX.X, ALU.add))
                settle()
                step(V.tensor_tensor(yrow[:, t % 2], sel2[:], rankK[:, t], ALU.add))
                settle()
                v.sem_inc(s_yr, 1)

            v.wait_ge(s_ic, 1)
            rows(0)
            rows(1)
            v.wait_ge(s_g2, 32)
            for t in range(NT):
                s = t % 2
                v.wait_ge(s_cl[s], 32 * (t // 2 + 1))
                if t >= 2:
                    v.wait_ge(s_out[s], 16 * (t // 2))
                v.wait_ge(s_yg[s], 16 * K * (t // 2 + 1))
                step(V.scalar_tensor_tensor(acc[:, s], x1c[:, s], ALPHA, xsh[:, s], ALU.mult, ALU.add))
                for k in range(K):
                    settle()
                    step(V.scalar_tensor_tensor(acc[:, s], yg[:, s, k], gates[:, t, k:k + 1], acc[:, s],
                                                ALU.mult, ALU.add))
                settle()
                v.sem_inc(s_acc, 1)
                if t + 2 < NT:
                    rows(t + 2)
                for b in range(2):
                    step(V.bn_stats(stat[:, 0, b], acc[:, s, b * 512:(b + 1) * 512]))
                settle()
                step(V.bn_aggr(mv[:, 0], stat[:, 0].rearrange("p a b -> p (a b)")))
                settle()
                V.tensor_scalar(mv[:, 0, 1:2], mv[:, 0, 1:2], EPS, None, ALU.add).then_inc(s_pv, 1)
                v.wait_ge(s_pw, NT + 2 + t)
                V.scalar_tensor_tensor(rs[:, 1:2], mv[:, 0, 0:1], -1.0, rs[:, 0:1], ALU.mult,
                                       ALU.mult).then_inc(s_nr, 1)
                v.wait_ge(s_hat, NT + t + 1)
                step(V.tensor_tensor(acc[:, s], acc[:, s], g2[:], ALU.mult))
                settle()
                V.tensor_tensor(acc[:, s], acc[:, s], b2[:], ALU.add).then_inc(s_o, 1)

        @block.tensor
        def _(pe):
            mm = nc.tensor.matmul

            def transpose_tile(src, bank):
                for c in range(ND):
                    last = nc.tensor.transpose(ps[:, bank + c // 4, (c % 4) * 128:(c % 4 + 1) * 128],
                                               src[:, c * 128:(c + 1) * 128], ident[:])
                return last

            pe.wait_ge(s_iden, 1)
            for t in range(NT):
                pe.wait_ge(s_x[t % 3], 16 * (t // 3 + 1))
                if t >= 2:
                    pe.wait_ge(s_xlo, t - 1)
                transpose_tile(xin[:, t % 3], 2 * (t % 2)).then_inc(s_xt, 1)
            for j, w in enumerate(JOBS):
                b = result(j)
                wait_result_free(pe, j)
                if w in W_JOBS:
                    n = W_JOBS.index(w)
                    pe.wait_ge(s_wlo, n + 1)
                    wt = whl[:, n % 2]
                if w == "gate0":
                    pe.wait_ge(s_xlo, NT)
                if w == "K0":
                    pe.wait_ge(s_mlo, 2)
                if w in WCOL:
                    for h in range(2):
                        for d in range(ND):
                            for st, mo in PRODS:
                                last = mm(ps[:, b + h, :], wt[:, st, d], xT[:, mo, d, h * 512:(h + 1) * 512],
                                          start=(d == 0 and st == 0 and mo == 0), stop=(d == ND - 1 and st == 1))
                elif w[0] == "K":
                    for d in range(ND):
                        for st, mo in PRODS:
                            last = mm(ps[:, b, 0:M], wt[:, st, d], memT[:, mo, d],
                                      start=(d == 0 and st == 0 and mo == 0), stop=(d == ND - 1 and st == 1))
                elif w[0] == "V":
                    for m in range(2):
                        for d in range(ND):
                            for st, mo in PRODS:
                                last = mm(ps[:, b, m * 128:(m + 1) * 128], memT[:, st, d, m * 128:(m + 1) * 128],
                                          wt[:, mo, d], start=(d == 0 and st == 0 and mo == 0),
                                          stop=(d == ND - 1 and st == 1))
                elif w[:4] == "pool":
                    c = int(w[4])
                    pe.wait_ge(s_diff, 1)
                    pe.wait_ge(s_bd, 64)
                    for h in range(2):
                        last = mm(ps[:, b + h, :], bd[:, c], diff[:, c, h * 512:(h + 1) * 512], start=True, stop=True)
                elif w in ("mean", "var"):
                    pe.wait_ge(s_const, 8)
                    pe.wait_ge(s_cvd if w == "mean" else s_sq, 1)
                    src = cv if w == "mean" else buf1
                    for h in range(2):
                        for c in range(2):
                            last = mm(ps[:, b + h, :], ones[:], src[:, c, h * 512:(h + 1) * 512],
                                      start=(c == 0), stop=(c == 1))
                last.then_inc(s_job, 1)
                if w == "gate0":
                    for m in range(2):
                        pe.wait_ge(s_mln, m + 1)
                        transpose_tile(memin[:, m], 2 * m).then_inc(s_mt, 1)
            pe.wait_ge(s_job, len(JOBS))
            pe.sem_inc(s_endP, 1)
            pe.wait_ge(s_endP, 4)

            pe.wait_ge(s_wrl, 1)
            pe.wait_ge(s_wolo, 4)
            for t in range(NT + 2):
                if t < NT:
                    pe.wait_ge(s_stl, t + 1)
                    if t >= 1:
                        pe.wait_ge(s_exp, 4 * t)
                    for h in range(HEADS):
                        for st, mo in PRODS:
                            last = mm(ps[:, h // 2, (h % 2) * M:(h % 2 + 1) * M], qst[:, t % 2, st, h], kT[:, mo, h],
                                      start=(st == 0 and mo == 0), stop=(st == 1))
                    last.then_inc(s_S, 1)
                if 1 <= t <= NT:
                    pe.wait_ge(s_olo, 2 * t)
                    if t >= 2:
                        pe.wait_ge(s_pre, t - 1)
                    for h in range(2):
                        for c in range(8):
                            for st, mo in PRODS:
                                last = mm(ps[:, 5 + h, :], mst[:, st, c], wo[:, mo, c, h * 512:(h + 1) * 512],
                                          start=(c == 0 and st == 0 and mo == 0), stop=(c == 7 and st == 1))
                    last.then_inc(s_pre_pe, 1)
                if t < NT:
                    if t >= 2:
                        pe.wait_ge(s_x1lo, 2 * (t - 1))
                    for h in range(HEADS):
                        pe.wait_ge(s_p, 4 * t + h + 1)
                        for m in range(2):
                            c = 2 * h + m
                            last = nc.tensor.transpose(ps[:, 2 + c // 4, (c % 4) * 128:(c % 4 + 1) * 128],
                                                       pr[:, h, m * 128:(m + 1) * 128], ident[:])
                        if h % 2:
                            last.then_inc(s_pt, 1)
                    pe.wait_ge(s_ptlo, 2 * t + 2)
                    if t >= 1:
                        pe.wait_ge(s_olo, 2 * t)
                    for h in range(HEADS):
                        for m in range(2):
                            for st, mo in PRODS:
                                last = mm(ps[:, 4, h * 128:(h + 1) * 128], vv[:, st, m, h * 128:(h + 1) * 128],
                                          pT[:, mo, 2 * h + m], start=(m == 0 and st == 0 and mo == 0),
                                          stop=(m == 1 and st == 1))
                    last.then_inc(s_ot, 1)
                if t >= 2:
                    u = t - 2
                    pe.wait_ge(s_mask, u + 1)
                    mm(ps[:, 7, 128:128 + E], tri[:], maskb[:], start=True, stop=False)
                    mm(ps[:, 7, 128:128 + E], oneb[:], cumb[:, u % 2], start=False, stop=True).then_inc(s_rk, 1)
                if 1 <= t <= NT:
                    u = t - 1
                    pe.wait_ge(s_x1, u + 1)
                    transpose_tile(xres[:, u % 2], 2).then_inc(s_tr, 1)
                    pe.wait_ge(s_x1lo, 2 * u + 2)
                    if u >= 1:
                        pe.wait_ge(s_rkc, u)
                    for d in range(ND):
                        for st, mo in PRODS:
                            last = mm(ps[:, 7, 0:E], x1T[:, st, d], wrt[:, mo, d],
                                      start=(d == 0 and st == 0 and mo == 0), stop=(d == ND - 1 and st == 1))
                    last.then_inc(s_lg, 1)
            pe.wait_ge(s_cumf, 1)
            mm(ps[:, 7, 128:128 + E], oneb[:], cumb[:, 0], start=True, stop=True).then_inc(s_cnt, 1)
            pe.wait_ge(s_cnt, 1)
            pe.sem_inc(s_endT, 1)
            if only_x1:
                return
            pe.wait_ge(s_endT, 4)
            pe.wait_ge(s_cm, 1)
            for f in range(3):
                for b in range(2):
                    c = 2 * f + b
                    last = mm(ps[0:1, 4 + c // 4, (c % 4) * 128:(c % 4 + 1) * 128], tabf[:, f, b:b + 1], ident[:],
                              start=True, stop=True)
            last.then_inc(s_tabp, 1)

            def rows_transposed(s):
                transpose_tile(xg[:, s], 0).then_inc(s_et, 1)

            pe.wait_ge(s_xg[0], 16)
            rows_transposed(0)

            def gate_up(s, slot):
                w = bass.ds(slot, 1)
                for d in range(ND):
                    for st, mo in PRODS:
                        last = mm(ps[:, 2 + s, :], xTe[:, s, st, d],
                                  wgu[:, w, mo, d].rearrange("p a n -> p (a n)"),
                                  start=(d == 0 and st == 0 and mo == 0), stop=(d == ND - 1 and st == 1))
                last.then_inc(s_gu, 1)

            def down(s, slot):
                w = bass.ds(slot, 1)
                for h in range(2):
                    for c in range(2):
                        for st, mo in PRODS:
                            last = mm(ps[:, 5 + h, :], hT[:, s, st, c],
                                      wdn[:, w, mo, c, h * 512:(h + 1) * 512].rearrange("p a n -> p (a n)"),
                                      start=(c == 0 and st == 0 and mo == 0), stop=(c == 1 and st == 1))
                last.then_inc(s_dn, 1)

            def step_pe(i, s, nth_next, jj=None):
                first = isinstance(i, int)
                e = 0 if first else pe.value_load(tab[0:1, 0, bass.ds(i, 1)], min_val=0, max_val=E)
                pe.wait_ge(s_xg[1 - s], 16 * nth_next)
                pe.wait_ge(s_elo, i + 1)
                rows_transposed(1 - s)
                pe.wait_ge(s_glo, 2 * e + 2)
                gate_up(s, e % 2)
                if not first:
                    ep = pe.value_load(tab[0:1, 0, bass.ds(i - 1, 1)], min_val=0, max_val=E)
                    pe.wait_ge(s_hlo, i)
                    pe.wait_ge(s_dlo, ep + 1)
                    if s == 0:
                        pe.wait_ge(s_y, 2 * i - 2)
                    else:
                        with pe.If(jj > 0):
                            pe.wait_ge(s_y, 2 * i - 2)
                            pe.sem_inc(s_seen, 1)
                    down(1 - s, ep % 2)
                pe.wait_ge(s_h, i + 1)
                for c in range(2):
                    last = nc.tensor.transpose(ps[:, 4, c * 128:(c + 1) * 128], hx[:, s, c * 128:(c + 1) * 128],
                                               ident[:])
                last.then_inc(s_ht, 1)

            pe.wait_ge(s_tabs, 1)
            n_items = pe.value_load(nit[0:1, 0:1], min_val=NT + E, max_val=MAX_ITEMS)
            step_pe(0, 0, 1)
            with pe.Fori(0, (STEPS - 1) // 2) as jj:
                with pe.If(n_items > 2 * jj):
                    step_pe(2 * jj + 1, 1, jj + 2, jj)
                with pe.If(n_items > 2 * jj + 1):
                    step_pe(2 * jj + 2, 0, jj + 2, jj)
            pe.wait_ge(s_ht, n_items + 1)
            pe.sem_inc(s_endR, 1)


CONST = {}


def pool_edges():
    import numpy as np
    t = np.concatenate([np.arange(8), np.arange(S - 8, S)])
    e = np.zeros((128, 2, 16), np.float32)
    for g, w in enumerate(POOL_WINDOWS):
        cnt = np.minimum(t - w // 2 + w, S) - np.maximum(t - w // 2, 0)
        e[64 * (g % 2):64 * (g % 2) + 64, g // 2, :] = 1.0 / cnt
    return e


def layouts(i):
    import numpy as np
    i = {k: np.asarray(v) for k, v in i.items()}
    c = lambda x: np.ascontiguousarray(x)
    cols = lambda w: c(w.reshape(ND, 128, -1, 128).transpose(2, 1, 0, 3))
    pch = lambda v: v.reshape(-1, 128).T
    ex = lambda w, k: c(w.reshape(-1, k, 128, w.shape[-1]).transpose(0, 2, 1, 3).reshape(-1, 128, 2048))
    return {
        "x": c(i["x"].reshape(NT, 128, D)), "mem": c(i["mem"].reshape(2, 128, D)),
        "w_in": cols(i["w_in"][0]), "w_kv": cols(i["w_kv"][0]),
        "mem_gb": c(np.stack([pch(i["mem_norm_g"]), pch(i["mem_norm_b"])], 1)),
        "w_dw": c(i["w_dw"][0].T.reshape(2, 128, TAPS).transpose(1, 0, 2)),
        "cpar": c(np.stack([pch(i[k][0]) for k in ("b_dw", "conv_norm_g", "conv_norm_b", "pool_scale")], 1)),
        "edge": pool_edges(), "w_pool": c(i["w_pool"][0]),
        "w_out": c(i["w_out"][0].reshape(4, 2, 128, D).transpose(0, 2, 1, 3).reshape(4, 128, 2 * D)),
        "ln1_g": c(i["ln1_g"]), "ln1_b": c(i["ln1_b"]), "ln2_g": c(i["ln2_g"]), "ln2_b": c(i["ln2_b"]),
        "router_bias": c(i["router_bias"]),
        "w_router": c(i["w_router"][0].reshape(ND, 128, E).transpose(1, 0, 2)),
        "sh_gate": ex(i["w_gate_sh"], ND)[0], "sh_up": ex(i["w_up_sh"], ND)[0], "sh_down": ex(i["w_down_sh"], 2)[0],
        "w_gate": ex(i["w_gate"][0], ND), "w_up": ex(i["w_up"][0], ND), "w_down": ex(i["w_down"][0], 2),
    }


ONLY_X1 = False


def kernel(**inputs):
    import numpy as np
    import concourse.bacc as bacc
    from concourse.bass_utils import run_bass_kernel_spmd

    nc = bacc.Bacc("TRN2", target_bir_lowering=False, num_devices=1)
    arrays, aps = {}, {}
    for name, v in layouts(inputs).items():
        arrays[f"in_{name}"] = v
        aps[name] = nc.dram_tensor(f"in_{name}", v.shape, mybir.dt.from_np(v.dtype), kind="ExternalInput").ap()
    out = nc.dram_tensor("out", (S, D), F, kind="ExternalOutput").ap()
    build(nc, aps, out, ONLY_X1)
    r = run_bass_kernel_spmd(nc, [arrays], core_ids=[0])
    return np.asarray(r.results[0]["out"]).reshape(1, S, D)
```

```python
import concourse.bass as bass
from concourse import mybir
from contextlib import ExitStack

F = mybir.dt.float32
R = mybir.dt.float32r
BF = mybir.dt.bfloat16
I32 = mybir.dt.int32
U32 = mybir.dt.uint32
ALU = mybir.AluOpType
ACT = mybir.ActivationFunctionType
AX = mybir.AxisListType

S = 1024
D = 1024
NT = S // 128
ND = D // 128
POOL_WINDOWS = (2, 4, 8, 16)
TAPS = 31
PAD = TAPS // 2
M = 256
HEADS = 4
DH = 128
E = 64
K = 8
XD = 256
NE = E + 1
MAX_ITEMS = NT + E + (S * K - E) // 128
PAIRS = (MAX_ITEMS - NT + 2) // 2
GROUP = 8
GROUPS = -(-PAIRS // GROUP)
TAB = 160
LIST = NE * S + 128 * 160
EPS = 1e-5
ALPHA = float(2 ** 0.25)
SCALE = float(DH) ** -0.5
ROUTED = 2.5
PRODS = ((0, 0), (0, 1), (1, 0))
KB = 1024


def build(nc, a, out):
    ctx = ExitStack()
    base = 16512

    def at(name, kb, shape, dt=F):
        return nc.alloc_sbuf_tensor_at(name, shape, dt, offset=base + int(kb * KB))

    def sem(name):
        return ctx.enter_context(nc.semaphore(name))

    with ctx:
        xT = at("xT", 0, [128, 2, ND, S], R)
        wo = at("wo", 0, [128, 2, 8, D], R)
        wgu = at("wgu", 0, [128, 2, 2, ND, 512], R)
        wdn = at("wdn", 64, [128, 2, 2, 2, D], R)
        qT = at("qT", 64, [128, HEADS, S])
        memin = at("memin", 64, [128, 2, D])
        mixA = at("mixA", 80, [128, 4, S])
        memT = at("memT", 80, [128, 2, ND, M], R)
        kT = at("kT", 96, [128, 2, HEADS, M], R)
        vv = at("vv", 104, [128, 2, 2, 512], R)
        xTe = at("xTe", 96, [128, 2, 2, ND, 128], R)
        raw = at("raw", 112, [128, 2, 3, 2048])
        wraw = at("wraw", 112, [128, 3, ND, 128])
        xin = at("xin", 124, [128, 3, D])
        whl = at("whl", 136, [128, 2, 2, ND, 128], R)
        uP = at("uP", 152, [128, 2, S + 16])
        glu = at("glu", 160.25, [128, 2, S + 32])
        cv = at("cv", 168.5, [128, 2, S])
        buf1 = at("buf1", 176.5, [128, 2, S + 16])
        buf2 = at("buf2", 184.75, [128, 2, S + 16])
        diff = at("diff", 193, [128, 2, S])
        mtmp = at("mtmp", 124, [128, ND, M])
        zero = at("zero", 201, [128, 512])
        mst = at("mst", 136, [128, 2, 2, 8, 128], R)
        qst = at("qst", 144, [128, 2, 2, HEADS, 128], R)
        pT = at("pT", 112, [128, 2, 8, 512], R)
        x1T = at("x1T", 152, [128, 2, ND, 128], R)
        xres = at("xres", 160, [128, 2, D])
        g1 = at("g1", 168, [128, D])
        b1 = at("b1", 172, [128, D])
        wrr = at("wrr", 180, [128, ND, E])
        wrt = at("wrt", 176, [128, 2, ND, E], R)
        pr = at("pr", 184, [128, 2, HEADS, M])
        oh = at("oh", 192, [128, K, E])
        ohx = at("ohx", 194, [128, K, E])
        sc = at("sc", 196, [128, E])
        sb_ = at("sb_", 196.25, [128, E])
        rbias = at("rbias", 196.75, [128, E])
        iotaE = at("iotaE", 197, [128, E])
        maskb = at("maskb", 197.25, [128, E], BF)
        maskf = at("maskf", 197.5, [128, E])
        cumb = at("cumb", 197.75, [128, 2, E], BF)
        cumf = at("cumf", 198, [128, E])
        top8 = at("top8", 198.25, [128, 8])
        idxu = at("idxu", 198.3125, [128, 8], U32)
        sel = at("sel", 198.375, [128, 8])
        addrf = at("addrf", 198.4375, [128, 8])
        addr = at("addr", 198.5, [128, 2, 8], U32)
        xg = at("xg", 160, [128, 2, D])
        hs = at("hs", 168, [128, 2, XD])
        hx = at("hx", 170, [128, 2, XD])
        hT = at("hT", 172, [128, 2, 2, 2, 128], R)
        ysb = at("ysb", 176, [128, 2, D])
        idx = at("idx", 184, [128, 2], U32)
        cmp_ = at("cmp_", 192, [128, 2, NE])
        cmpx = at("cmpx", 193, [128, 2, NE])
        tabf = at("tabf", 194, [128, 3, 2])
        tab = at("tab", 185, [1, 3, TAB], I32)
        nit = at("nit", 188.25, [1, 8], I32)
        yg = at("yg", 0, [128, 2, K, D])
        xsh = at("xsh", 64, [128, 2, D])
        x1c = at("x1c", 72, [128, 2, D])
        acc = at("acc", 80, [128, 2, D])
        g2 = at("g2", 96, [128, D])
        b2 = at("b2", 100, [128, D])
        diag = at("diag", 104, [128, 2, K // 2, 128])
        yrow = at("yrow", 188.5, [128, NT, K], U32)
        epst = at("epst", 207.71875, [128, 1])
        neghalf = at("neghalf", 207.6875, [128, 2])
        ident = at("ident", 203, [128, 128])
        tri = at("tri", 203.5, [128, 128], BF)
        oneb = at("oneb", 203.75, [128, 128], BF)
        ones = at("ones", 204, [128, 128])
        bd = at("bd", 204.5, [128, 2, 128])
        mgb = at("mgb", 205.5, [128, 2, ND])
        wdw = at("wdw", 205.5625, [128, 2, TAPS])
        cpar = at("cpar", 205.875, [128, 4, 2])
        edge = at("edge", 205.9375, [128, 2, 16])
        gates = at("gates", 206.0625, [128, NT, K])
        idxf = at("idxf", 206.3125, [128, NT, K])
        rankK = at("rankK", 206.5625, [128, NT, K])
        stat = at("stat", 206.8125, [128, 2, 2, 6])
        mv = at("mv", 206.90625, [128, 2, 2])
        sm = at("sm", 192, [128, 2, 3, HEADS])
        tok = at("tok", 207, [128, 2], U32)
        tokf = at("tokf", 207.03125, [128, 2])
        rs = at("rs", 207.0625, [128, 4])
        gs = at("gs", 207.09375, [128, 4])
        startE = at("startE", 207.125, [128, NE])
        endE = at("endE", 207.40625, [128, NE])
        fillw = at("fillw", 200.4375, [128, 96], U32)
        cnt65 = at("cnt65", 198.625, [128, NE])
        blk = at("blk", 199, [128, NE])
        blki = at("blki", 199.375, [128, NE], I32)
        itemp = at("itemp", 199.75, [128, 2])
        ones65 = at("ones65", 200, [128, NE])
        idlist = at("idlist", 200.375, [128, 8], U32)

        ps = ctx.enter_context(nc.psum_tensor("ps", [128, 8, 512], F))

        x1_d = nc.dram_tensor("x1_d", [S, D], F, kind="Internal").ap()
        list_d = nc.dram_tensor("list_d", [LIST, 1], U32, kind="Internal").ap()
        y_d = nc.dram_tensor("y_d", [(MAX_ITEMS + 1) * 128, D], F, kind="Internal").ap()

        s_const = sem("s_const")
        s_iden = sem("s_iden")
        s_pool = sem("s_pool")
        s_par = sem("s_par")
        s_bd = sem("s_bd")
        s_x = [sem(f"s_xin{i}") for i in range(3)]
        s_mem = sem("s_mem")
        s_w = [sem(f"s_w{i}") for i in range(3)]
        s_wo = [sem(f"s_wo{n}") for n in range(4)]
        s_xt = sem("s_xt")
        s_xhi = sem("s_xhi")
        s_xlo = sem("s_xlo")
        s_whi = sem("s_whi")
        s_wlo = sem("s_wlo")
        s_job = sem("s_job")
        s_gfree = [sem("s_g0"), sem("s_g1")]
        s_sig = sem("s_sig")
        s_glu = sem("s_glu")
        s_u = sem("s_u")
        s_diff = sem("s_diff")
        s_mln = sem("s_mln")
        s_mt = sem("s_mt")
        s_mtc = sem("s_mtc")
        s_mhi = sem("s_mhi")
        s_mlo = sem("s_mlo")
        s_kvhi = sem("s_kvhi")
        s_v = sem("s_v")
        s_cvd = sem("s_cvd")
        s_yc = sem("s_yc")
        s_sq = sem("s_sq")
        s_sd = sem("s_sd")
        s_yn = sem("s_yn")
        s_mix = sem("s_mix")
        s_wohi, s_wolo = sem("s_wohi"), sem("s_wolo")
        s_pv = sem("s_pv")
        s_pw = sem("s_pw")
        s_endP = sem("s_endP")
        s_fill = sem("s_fill")
        s_zero = sem("s_zero")
        s_pt2 = sem("s_pt2")
        s_st, s_stl = sem("s_st"), sem("s_stl")
        s_S = sem("s_S")
        s_negm = sem("s_negm")
        s_exp = sem("s_exp")
        s_p = sem("s_p")
        s_pt = sem("s_pt")
        s_pthi, s_ptlo = sem("s_pthi"), sem("s_ptlo")
        s_ot = sem("s_ot")
        s_oe = sem("s_oe")
        s_gb = sem("s_gb")
        s_wr = sem("s_wr")
        s_wrhi, s_wrl = sem("s_wrhi"), sem("s_wrl")
        s_xr = (sem("s_xr0"), sem("s_xr1"))
        s_ohi, s_olo = sem("s_ohi"), sem("s_olo")
        s_pre_h, s_pre_pe = sem("s_pre_h"), sem("s_pre_pe")
        s_pre = sem("s_pre")
        s_mr = sem("s_mr")
        s_hat = sem("s_hat")
        s_x1 = sem("s_x1")
        s_x1w = (sem("s_x1w0"), sem("s_x1w1"))
        s_tr = sem("s_tr")
        s_x1hi, s_x1lo = sem("s_x1hi"), sem("s_x1lo")
        s_lg = sem("s_lg")
        s_scr = sem("s_scr")
        s_scu = sem("s_scu")
        s_mask = sem("s_mask")
        s_rk = sem("s_rk")
        s_rkc = sem("s_rkc")
        s_addr = sem("s_addr")
        s_sc = (sem("s_sc0"), sem("s_sc1"))
        s_cumf = sem("s_cumf")
        s_cnt = sem("s_cnt")
        s_cm = sem("s_cm")
        s_tabp = sem("s_tabp")
        s_tabs = sem("s_tabs")
        s_seen = sem("s_seen")
        s_rw = (sem("s_rw0"), sem("s_rw1"))
        s_rwd = (sem("s_rwd0"), sem("s_rwd1"))
        s_ready = sem("s_ready")
        s_dready = sem("s_dready")
        s_ghi, s_glo = sem("s_ghi"), sem("s_glo")
        s_dhi, s_dlo = sem("s_dhi"), sem("s_dlo")
        s_xs = (sem("s_xs0"), sem("s_xs1"))
        s_idx = (sem("s_idx0"), sem("s_idx1"))
        s_xg = (sem("s_xg0"), sem("s_xg1"))
        s_et = sem("s_et")
        s_ehi, s_elo = sem("s_ehi"), sem("s_elo")
        s_gu = sem("s_gu")
        s_silu = sem("s_silu")
        s_h = sem("s_h")
        s_ht = sem("s_ht")
        s_hhi, s_hlo = sem("s_hhi"), sem("s_hlo")
        s_dn = sem("s_dn")
        s_y = sem("s_y")
        s_yd = (sem("s_yd0"), sem("s_yd1"))
        s_ylast = sem("s_ylast")
        s_endR = sem("s_endR")
        s_cl = (sem("s_cl0"), sem("s_cl1"))
        s_g2 = sem("s_g2")
        s_yg = tuple((sem(f"s_yg{s}a"), sem(f"s_yg{s}b")) for s in range(2))
        s_dg = sem("s_dg")
        s_pc = sem("s_pc")
        s_acc = sem("s_acc")
        s_nr = sem("s_nr")
        s_o = sem("s_o")
        s_out = (sem("s_out0"), sem("s_out1"))

        W_JOBS = ["gate0", "a0", "gate1", "a1", "u0", "u1", "K0", "K1", "K2", "K3",
                  "V0", "V1", "V2", "V3", "q0", "q1", "q2", "q3"]
        JOBS = W_JOBS[:15] + ["pool0", "pool1"] + W_JOBS[15:17] + ["mean", "q3", "var"]
        WCOL = {"gate0": 4, "a0": 2, "gate1": 5, "a1": 3, "u0": 0, "u1": 1,
                "q0": 6, "q1": 7, "q2": 8, "q3": 9}
        TAPS_IN = {"u0": 10, "u1": 10, "q0": 9, "q1": 9, "q2": 8}
        TAPS_IN.update({w: 2 for w in W_JOBS[6:14]})
        taps = [(k, c) for k in range(TAPS) for c in range(2)]

        def w_src(n):
            w = W_JOBS[n]
            if w in WCOL:
                return a["w_in"][WCOL[w]]
            return a["w_kv"][int(w[1]) + (4 if w[0] == "V" else 0)]

        def result(j):
            return 4 + 2 * (j % 2)

        def wait_result_free(eng, j):
            if j >= 2:
                eng.wait_ge(s_gfree[j % 2], j // 2)

        def rank_bank(u):
            return 0 if u < NT - 2 else 7

        block = ctx.enter_context(nc.Block())

        @block.sync
        def _(sp):
            sp.dma_start(mgb[:], a["mem_gb"]).then_inc(s_par, 16)
            sp.dma_start(wdw[:], a["w_dw"]).then_inc(s_par, 16)
            sp.dma_start(cpar[:], a["cpar"]).then_inc(s_par, 16)
            sp.dma_start(edge[:], a["edge"]).then_inc(s_par, 16)
            sp.wait_ge(s_const, 1)
            for g in range(4):
                o = 64 * (g % 2)
                sp.dma_start(bd[o:o + 64, g // 2, o:o + 64], a["w_pool"][g]).then_inc(s_bd, 16)
            for n in range(18):
                if n >= 3:
                    sp.wait_ge(s_wlo, n - 2)
                sp.dma_start(wraw[:, n % 3], w_src(n)).then_inc(s_w[n % 3], 16)
                if n == 2:
                    for m in range(2):
                        sp.dma_start(memin[:, m], a["mem"][m]).then_inc(s_mem, 16)
            sp.wait_ge(s_wlo, 18)
            sp.wait_ge(s_job, JOBS.index("q3") + 1)
            for n in range(4):
                sp.dma_start(raw[:, n // 3, n % 3], a["w_out"][n]).then_inc(s_wo[n], 16)
            sp.wait_ge(s_endP, 4)
            for dst, src in ((g1, "ln1_g"), (b1, "ln1_b"), (rbias, "router_bias")):
                sp.dma_start(dst[:], a[src].to_broadcast([128, dst.shape[1]])).then_inc(s_gb, 16)
            sp.dma_start(wrr[:], a["w_router"]).then_inc(s_wr, 16)
            for t in range(2):
                sp.dma_start(xres[:, t], a["x"][t]).then_inc(s_xr[t], 16)
            def zero_rows(n):
                n = NT + E + 8 * n
                for h in range(2):
                    sp.dma_start(y_d[n * 128:(n + 8) * 128, h * 512:(h + 1) * 512].rearrange("(i p) d -> p i d", p=128),
                                 zero[:].unsqueeze(1).to_broadcast([128, 8, 512])).then_inc(s_zero, 16)

            for n in range(5):
                zero_rows(n)
            sp.wait_ge(s_ot, 2 * HEADS)
            for n, w in enumerate(("sh_gate", "sh_up", "sh_down")):
                sp.dma_start(raw[:, 0, n], a[w]).then_inc(s_rwd[0] if n == 2 else s_rw[0], 16)
            sp.wait_ge(s_rw[0], 32)
            sp.sem_inc(s_ready, 1)
            sp.wait_ge(s_rwd[0], 16)
            sp.sem_inc(s_dready, 1)
            for t in range(NT):
                sp.wait_ge(s_x1, t + 1)
                sp.dma_start(x1_d[t * 128:(t + 1) * 128, :], xres[:, t % 2]).then_inc(s_x1w[t % 2], 16)
                if t < 3:
                    zero_rows(5 + t)
                if t == NT - 2:
                    sp.wait_ge(s_x1w[0], 16 * 4)
                    sp.wait_ge(s_tr, NT - 1)
                    sp.dma_start(xg[:, 0], x1_d[0:128, :]).then_inc(s_xs[0], 16)
                if t + 2 < NT:
                    sp.wait_ge(s_x1w[t % 2], 16 * (t // 2 + 1))
                    sp.wait_ge(s_tr, t + 1)
                    sp.dma_start(xres[:, t % 2], a["x"][t + 2]).then_inc(s_xr[t % 2], 16)
            sp.wait_ge(s_tr, NT)
            sp.wait_ge(s_x1w[1], 16 * 4)
            sp.dma_start(xg[:, 1], x1_d[128:256, :]).then_inc(s_xs[1], 16)
            sp.wait_ge(s_pre_pe, NT)
            sp.wait_ge(s_lg, NT)
            sp.dma_start(raw[:, 1, 0], a["w_gate"][0]).then_inc(s_rw[1], 16)
            sp.dma_start(raw[:, 1, 1], a["w_up"][0]).then_inc(s_rw[1], 16)
            sp.dma_start(raw[:, 1, 2], a["w_down"][0]).then_inc(s_rwd[1], 16)

            def load_expert(e, s, nth):
                def load(w, n, done):
                    sp.dma_start(raw[:, s, n], a[w][bass.ds(e - 1, 1)].rearrange("a p n -> (a p) n")).then_inc(done, 16)
                sp.wait_ge(s_glo, 2 * e - 2)
                load("w_gate", 0, s_rw[s])
                load("w_up", 1, s_rw[s])
                sp.wait_ge(s_rw[1 - s], 32 * nth)
                sp.sem_inc(s_ready, 1)
                sp.wait_ge(s_dlo, e - 1)
                load("w_down", 2, s_rwd[s])
                sp.wait_ge(s_rwd[1 - s], 16 * nth)
                sp.sem_inc(s_dready, 1)

            for i in range(2, NT):
                sp.wait_ge(s_et, i - 1)
                sp.dma_start(xg[:, i % 2], x1_d[i * 128:(i + 1) * 128, :]).then_inc(s_xs[i % 2], 16)
                if i == 2:
                    load_expert(2, 0, 1)
            load_expert(3, 1, 2)
            with sp.Fori(0, 30) as jj:
                load_expert(2 * jj + 4, 0, jj + 2)
                load_expert(2 * jj + 5, 1, jj + 3)
            load_expert(64, 0, 32)
            sp.wait_ge(s_rw[0], 32 * 33)
            sp.sem_inc(s_ready, 1)
            sp.wait_ge(s_rwd[0], 16 * 33)
            sp.sem_inc(s_dready, 1)
            sp.wait_ge(s_endR, 4)
            for t in range(2):
                sp.dma_start(x1c[:, t], x1_d[t * 128:(t + 1) * 128, :]).then_inc(s_cl[t], 16)
                sp.dma_start(xsh[:, t], y_d[t * 128:(t + 1) * 128, :]).then_inc(s_cl[t], 16)
            sp.dma_start(g2[:], a["ln2_g"].to_broadcast([128, D])).then_inc(s_g2, 16)
            sp.dma_start(b2[:], a["ln2_b"].to_broadcast([128, D])).then_inc(s_g2, 16)
            for t in range(NT):
                s = t % 2
                if t + 2 < NT:
                    sp.wait_ge(s_acc, t + 1)
                    sp.wait_ge(s_pc, t + 1)
                    r = slice((t + 2) * 128, (t + 3) * 128)
                    sp.dma_start(x1c[:, s], x1_d[r, :]).then_inc(s_cl[s], 16)
                    sp.dma_start(xsh[:, s], y_d[r, :]).then_inc(s_cl[s], 16)
                sp.wait_ge(s_o, t + 1)
                sp.dma_start(out[t * 128:(t + 1) * 128, :], acc[:, s]).then_inc(s_out[s], 16)
            for s in range(2):
                sp.wait_ge(s_out[s], 16 * 4)

        @block.gpsimd
        def _(g):
            g.memset(bd[:], 0.0).then_inc(s_const, 1)
            for t in range(3):
                g.dma_start(xin[:, t], a["x"][t]).then_inc(s_x[t], 16)
            g.memset(zero[:], 0.0).then_inc(s_pool, 1)
            g.memset(ident[:], 0.0).then_inc(s_pool, 1)
            g.memset(tri[:], 1.0).then_inc(s_pool, 1)
            g.memset(ones[:], 1.0 / 256).then_inc(s_const, 1)
            g.memset(oneb[:], 1.0).then_inc(s_const, 1)
            g.memset(neghalf[:], -0.5).then_inc(s_pool, 1)
            g.memset(epst[:], EPS).then_inc(s_pool, 1)
            g.wait_ge(s_pool, 5)
            g.affine_select(out=ident[:], in_=ident[:], compare_op=ALU.not_equal, fill=1.0, base=0,
                            pattern=[[-1, 128]], channel_multiplier=1).then_inc(s_iden, 1)
            g.affine_select(out=tri[:], in_=tri[:], compare_op=ALU.is_gt, fill=0.0, base=0,
                            pattern=[[1, 128]], channel_multiplier=-1).then_inc(s_const, 1)
            g.memset(uP[:, :, 0:8], 0.0).then_inc(s_const, 1)
            g.memset(uP[:, :, S + 8:S + 16], 0.0).then_inc(s_const, 1)
            g.memset(glu[:, :, 0:PAD], 0.0).then_inc(s_const, 1)
            g.memset(glu[:, :, PAD + S:S + 32], 0.0).then_inc(s_const, 1)
            for t in range(3, NT):
                g.wait_ge(s_xt, t - 2)
                g.dma_start(xin[:, t % 3], a["x"][t]).then_inc(s_x[t % 3], 16)
            g.wait_ge(s_pv, 1)
            g.tensor_tensor(mv[:, :, 1], mv[:, :, 1], neghalf[:], ALU.pow).then_inc(s_pw, 1)
            g.wait_ge(s_u, 2)
            g.wait_ge(s_const, 8)
            n = 5
            W = S + 16

            def step(ins):
                nonlocal n
                ins.then_inc(s_pool, 1)
                n += 1
                g.wait_ge(s_pool, n)
            step(g.tensor_tensor(buf1[:, :, 0:W - 1], uP[:, :, 0:W - 1], uP[:, :, 1:W], ALU.add))
            step(g.tensor_tensor(buf2[:, :, 0:W - 3], buf1[:, :, 0:W - 3], buf1[:, :, 2:W - 1], ALU.add))

            def mean_minus_token(grp, buf):
                w = POOL_WINDOWS[grp]
                p, c, lo = slice(64 * (grp % 2), 64 * (grp % 2) + 64), grp // 2, 8 - w // 2
                step(g.tensor_scalar(diff[p, c, :], buf[p, c, lo:lo + S], 1.0 / w, None, ALU.mult))
                for t0, e0 in ((0, 0), (S - 8, 8)):
                    step(g.tensor_tensor(diff[p, c, t0:t0 + 8], buf[p, c, lo + t0:lo + t0 + 8],
                                         edge[p, c, e0:e0 + 8], ALU.mult))
                step(g.tensor_tensor(diff[p, c, :], diff[p, c, :], uP[p, c, 8:8 + S], ALU.subtract))
            g.wait_ge(s_par, 64)
            mean_minus_token(0, buf1)
            mean_minus_token(1, buf2)
            step(g.tensor_tensor(buf1[:, 1, 0:W - 7], buf2[:, 1, 0:W - 7], buf2[:, 1, 4:W - 3], ALU.add))
            mean_minus_token(2, buf1)
            step(g.tensor_tensor(buf2[:, 1, 0:W - 15], buf1[:, 1, 0:W - 15], buf1[:, 1, 8:W - 7], ALU.add))
            mean_minus_token(3, buf2)
            g.sem_inc(s_diff, 1)
            g.sem_inc(s_endP, 1)
            g.wait_ge(s_endP, 4)
            g.iota(iotaE[:], pattern=[[1, E]], base=0, channel_multiplier=0,
                   allow_small_or_imprecise_dtypes=True).then_inc(s_pt2, 1)
            g.iota(tokf[:], pattern=[[128, 2]], base=0, channel_multiplier=1,
                   allow_small_or_imprecise_dtypes=True).then_inc(s_pt2, 1)
            g.iota(itemp[:], pattern=[[128, 2]], base=0, channel_multiplier=1,
                   allow_small_or_imprecise_dtypes=True).then_inc(s_pt2, 1)
            g.iota(idlist[:], pattern=[[1, 8]], base=0, channel_multiplier=8).then_inc(s_pt2, 1)
            g.iota(fillw[:], pattern=[[0, 96]], base=2048, channel_multiplier=0).then_inc(s_pt2, 1)
            g.memset(ones65[:], 1.0).then_inc(s_pt2, 1)
            g.memset(cumf[:], 0.0).then_inc(s_pt2, 1)
            g.memset(cumb[:], 0.0).then_inc(s_pt2, 1)
            g.wait_ge(s_pt2, 8)
            g.dma_start(list_d[0:S, :].rearrange("(p j) a -> p (j a)", j=8), idlist[:]).then_inc(s_fill, 16)
            for n in range(7):
                g.dma_start(list_d[S + n * 12288:S + (n + 1) * 12288, :].rearrange("(p j) a -> p (j a)", p=128),
                            fillw[:]).then_inc(s_fill, 16)

            def rstd(n):
                g.wait_ge(s_pv, n)
                g.tensor_tensor(rs[:, 0:1], mv[:, 0, 1:2], neghalf[:, 0:1], ALU.pow).then_inc(s_pw, 1)

            def mix_lo(t):
                cols = slice(t * 128, (t + 1) * 128)
                for half, src in ((slice(0, 4), mixA), (slice(4, 8), qT)):
                    g.wait_ge(s_ohi, 2 * t + 1 + half.start // 4)
                    g.tensor_tensor(mst[:, t % 2, 1, half], src[:, :, cols],
                                    mst[:, t % 2, 0, half].bitcast(F), ALU.subtract).then_inc(s_olo, 1)

            def scatter(t):
                g.wait_ge(s_addr, t + 1)
                for k in range(K):
                    g.indirect_dma_start(
                        out=list_d, out_offset=bass.IndirectOffsetOnAxis(ap=addr[:, t % 2, k:k + 1], axis=0),
                        in_=tok[:, t % 2:t % 2 + 1], in_offset=None,
                        bounds_check=LIST - 1, oob_is_err=True).then_inc(s_sc[t % 2], 16)

            mix_lo(0)
            mix_lo(1)
            g.wait_ge(s_fill, 128)
            for t in range(NT + 2):
                if t < NT:
                    rstd(t + 2)
                if t + 2 < NT:
                    mix_lo(t + 2)
                if t >= 2:
                    scatter(t - 2)
            for s in range(2):
                g.wait_ge(s_sc[s], 16 * K * 4)
            for s in range(2):
                g.wait_ge(s_x1w[s], 16 * 4)
            g.wait_ge(s_tabs, 1)
            n_items = g.value_load(nit[0:1, 0:1], min_val=NT + E, max_val=MAX_ITEMS)

            def token_list(i, s):
                lb = g.value_load(tab[0:1, 2, bass.ds(i, 1)], min_val=0, max_val=LIST - 128)
                return lambda: g.dma_start(idx[:, s:s + 1], list_d[bass.ds(lb, 128), :]).then_inc(s_idx[s], 16)

            def gather(i, s, nth):
                g.wait_ge(s_idx[s], 16 * nth)
                g.wait_ge(s_et, i - 1)
                g.sem_inc(s_seen, 1)
                g.indirect_dma_start(
                    out=xg[:, s], out_offset=None, in_=x1_d,
                    in_offset=bass.IndirectOffsetOnAxis(ap=idx[:, s:s + 1], axis=0),
                    bounds_check=S - 1, oob_is_err=False).then_inc(s_xg[s], 16)

            def fetch(i, s, nth_next, nth):
                gather(i + 1, 1 - s, nth_next)
                load = token_list(i + 2, s)
                g.wait_ge(s_xg[s], 16 * nth)
                g.sem_inc(s_seen, 1)
                load()

            token_list(NT, 0)()
            token_list(NT + 1, 1)()
            gather(NT, 0, 1)
            with g.Fori(0, GROUPS) as group:
                with g.If(n_items > 2 * GROUP * group + NT - 1):
                    with g.Fori(0, GROUP) as pair:
                        jj = GROUP * group + pair
                        with g.If(n_items > 2 * jj + NT - 1):
                            fetch(2 * jj + NT, 0, jj + 1, jj + 1)
                            with g.If(n_items > 2 * jj + NT):
                                fetch(2 * jj + NT + 1, 1, jj + 2, jj + 1)
            g.wait_ge(s_et, n_items + 2)
            g.sem_inc(s_endR, 1)
            g.wait_ge(s_endR, 4)
            for t in range(NT):
                s = t % 2
                if t >= 2:
                    g.wait_ge(s_pc, t - 1)
                    g.wait_ge(s_acc, t - 1)
                for k in range(K):
                    g.indirect_dma_start(
                        out=yg[:, s, k], out_offset=None, in_=y_d,
                        in_offset=bass.IndirectOffsetOnAxis(ap=yrow[:, t, k:k + 1], axis=0),
                        bounds_check=MAX_ITEMS * 128 - 1, oob_is_err=True).then_inc(s_yg[s][k // (K // 2)], 16)
                if t >= 1:
                    rstd(NT + 1 + t)
            rstd(2 * NT + 1)
            for s in range(2):
                for half in range(2):
                    g.wait_ge(s_yg[s][half], 16 * (K // 2) * 4)

        @block.scalar
        def _(act):
            def split_hi(n):
                act.wait_ge(s_w[n % 3], 16 * (n // 3 + 1))
                if n >= 2:
                    j = JOBS.index(W_JOBS[n - 2])
                    act.wait_ge(s_job, j + 1)
                nc.scalar.copy(whl[:, n % 2, 0], wraw[:, n % 3]).then_inc(s_whi, 1)

            split_hi(0)
            for t in range(NT):
                act.wait_ge(s_xt, t + 1)
                for b in range(2):
                    nc.scalar.copy(xT[:, 0, 4 * b:4 * b + 4, t * 128:(t + 1) * 128],
                                   ps[:, 2 * (t % 2) + b, :].rearrange("p (c n) -> p c n", c=4)).then_inc(s_xhi, 1)
            for j, w in enumerate(JOBS):
                s, b = j % 2, result(j)
                both = ps[:, b:b + 2, :].rearrange("p a n -> p (a n)")
                if w in W_JOBS and W_JOBS.index(w) < 17:
                    split_hi(W_JOBS.index(w) + 1)
                if w == "u1":
                    act.wait_ge(s_mtc, 1)
                    nc.scalar.copy(memT[:, 0, 0:4], mtmp[:, 0:4]).then_inc(s_mhi, 1)
                    nc.scalar.copy(memT[:, 0, 4:8], mtmp[:, 4:8]).then_inc(s_mhi, 1)
                if w != "mean" and w != "var":
                    act.wait_ge(s_job, j + 1)
                if w[:4] == "gate":
                    c = int(w[4])
                    nc.scalar.activation(glu[:, c, PAD:PAD + S], both, ACT.Sigmoid).then_inc(s_sig, 1)
                    act.wait_ge(s_sig, c + 1)
                    act.sem_inc(s_gfree[s], 1)
                elif w[0] == "u":
                    nc.scalar.copy(uP[:, int(w[1]), 8:8 + S], both).then_inc(s_u, 1)
                    act.wait_ge(s_u, int(w[1]) + 1)
                    act.sem_inc(s_gfree[s], 1)
                elif w[0] == "K":
                    nc.scalar.copy(kT[:, 0, int(w[1])], ps[:, b, 0:M]).then_inc(s_kvhi, 1)
                elif w[0] == "V":
                    c = int(w[1])
                    nc.scalar.copy(vv[:, 0, :, c * 128:(c + 1) * 128],
                                   ps[:, b, 0:256].rearrange("p (m n) -> p m n", m=2)).then_inc(s_kvhi, 1)
                elif w[0] == "q":
                    nc.scalar.copy(qT[:, int(w[1])], both).then_inc(s_gfree[s], 1)
                elif w[:4] == "pool":
                    c = int(w[4])
                    nc.scalar.activation(mixA[:, c], both, ACT.Copy, scale=cpar[:, 3, c:c + 1]).then_inc(s_gfree[s], 1)
                elif w == "mean":
                    act.wait_ge(s_yc, 1)
                    act.wait_ge(s_diff, 1)
                    nc.scalar.activation(buf1[:, :, 0:S], cv[:], ACT.Square).then_inc(s_sq, 1)
                elif w == "var":
                    act.wait_ge(s_job, j + 1)
                    nc.scalar.activation(buf2[:, 1, 0:S], both, ACT.Sqrt, bias=epst[:]).then_inc(s_sd, 1)
                    for n in range(4):
                        act.wait_ge(s_wo[n], 16)
                        nc.scalar.copy(wo[:, 0, 2 * n:2 * n + 2],
                                       raw[:, n // 3, n % 3].rearrange("p (c n) -> p c n", c=2)).then_inc(s_wohi, 1)
                    act.wait_ge(s_yn, 1)
                    for c in range(2):
                        nc.scalar.activation(mixA[:, 2 + c], cv[:, c], ACT.Silu, bias=cpar[:, 2, c:c + 1],
                                             scale=cpar[:, 1, c:c + 1]).then_inc(s_mix, 1)
            act.wait_ge(s_mix, 2)
            act.wait_ge(s_wohi, 4)
            act.sem_inc(s_endP, 1)
            act.wait_ge(s_endP, 4)


            def q_hi(t):
                if t >= 2:
                    act.wait_ge(s_S, t - 1)
                nc.scalar.copy(qst[:, t % 2, 0], qT[:, :, t * 128:(t + 1) * 128]).then_inc(s_st, 1)

            def exps(t):
                act.wait_ge(s_negm, t + 1)
                if t >= 2:
                    act.wait_ge(s_pt, 2 * (t - 1))
                for h in range(HEADS):
                    nc.scalar.activation(pr[:, t % 2, h], ps[:, 2 * (t % 2) + h // 2, (h % 2) * M:(h % 2 + 1) * M],
                                         ACT.Exp, bias=sm[:, t % 2, 0, h:h + 1], scale=SCALE,
                                         accum_out=sm[:, t % 2, 1, h:h + 1]).then_inc(s_exp, 1)

            def attention_out(g):
                act.wait_ge(s_stl, 4 * g + 4)
                for h in range(HEADS):
                    act.wait_ge(s_ot, 4 * g + h + 1)
                    nc.scalar.copy(qT[:, h, g * 512:(g + 1) * 512], ps[:, 6 + h % 2, :]).then_inc(s_oe, 1)

            q_hi(0)
            q_hi(1)
            exps(0)
            q_hi(2)
            for t in range(NT):
                if t + 1 < NT:
                    exps(t + 1)
                if t == 4:
                    attention_out(0)
                for b in range(2):
                    act.wait_ge(s_pt, 2 * t + b + 1)
                    nc.scalar.copy(pT[:, 0, 4 * b:4 * b + 4, (t % 4) * 128:(t % 4 + 1) * 128],
                                   ps[:, 4 + b, :].rearrange("p (c n) -> p c n", c=4)).then_inc(s_pthi, 1)
                if t + 3 < NT:
                    q_hi(t + 3)
            attention_out(1)
            act.wait_ge(s_oe, 2 * HEADS)

            def gate_up_hi(e, n):
                v = bass.ds(e % 2, 1)
                nc.scalar.copy(wgu[:, v, 0, :, n * XD:(n + 1) * XD].rearrange("p a c n -> p (a c) n"),
                               raw[:, v, n].rearrange("p a (c n) -> p (a c) n", c=ND)).then_inc(s_ghi, 1)

            def mix_hi(t):
                if t >= 2:
                    act.wait_ge(s_pre_pe, t - 1)
                cols = slice(t * 128, (t + 1) * 128)
                nc.scalar.copy(mst[:, t % 2, 0, 0:4], mixA[:, :, cols]).then_inc(s_ohi, 1)
                nc.scalar.copy(mst[:, t % 2, 0, 4:8], qT[:, :, cols]).then_inc(s_ohi, 1)

            mix_hi(0)
            mix_hi(1)
            act.wait_ge(s_wr, 16)
            nc.scalar.copy(wrt[:, 0], wrr[:]).then_inc(s_wrhi, 1)
            for t in range(NT + 1):
                if t >= 1:
                    act.wait_ge(s_tr, t)
                    if t >= 2:
                        act.wait_ge(s_lg, t - 1)
                    for b in range(2):
                        nc.scalar.copy(x1T[:, 0, 4 * b:4 * b + 4],
                                       ps[:, 2 + b, :].rearrange("p (c n) -> p c n", c=4)).then_inc(s_x1hi, 1)
                if t < NT:
                    act.wait_ge(s_mr, t + 1)
                    nc.scalar.activation(xres[:, t % 2], xres[:, t % 2], ACT.Identity,
                                         bias=rs[:, 1:2], scale=rs[:, 0:1]).then_inc(s_hat, 1)
                if t + 2 < NT:
                    mix_hi(t + 2)
                if t >= 1:
                    if t == NT:
                        act.wait_ge(s_pre_pe, NT)
                        act.wait_ge(s_ready, 1)
                        gate_up_hi(0, 0)
                        gate_up_hi(0, 1)
                    act.wait_ge(s_lg, t)
                    if t >= 2:
                        act.wait_ge(s_scu, t - 1)
                    nc.scalar.activation(sc[:], ps[:, 7, 0:E], ACT.Sigmoid).then_inc(s_scr, 1)
            act.wait_ge(s_zero, 32 * NT)

            def down_hi(e):
                v = bass.ds(e % 2, 1)
                nc.scalar.copy(wdn[:, v, 0].rearrange("p a c n -> p (a c) n"),
                               raw[:, v, 2].rearrange("p a (c n) -> p (a c) n", c=2)).then_inc(s_dhi, 1)

            def item_hi(i, s):
                act.wait_ge(s_et, i + 1)
                for b in range(2):
                    nc.scalar.copy(xTe[:, s, 0, 4 * b:4 * b + 4],
                                   ps[:, b, :].rearrange("p (c n) -> p c n", c=4)).then_inc(s_ehi, 1)

            def y_out(slot):
                for b in range(2):
                    nc.scalar.copy(ysb[:, slot, b * 512:(b + 1) * 512], ps[:, 5 + b, :]).then_inc(s_y, 1)

            item_hi(0, 0)
            act.sem_inc(s_yd[0], 16)
            act.sem_inc(s_yd[1], 16)
            act.sem_inc(s_y, 2)

            def step_act(i, s, nth):
                shared = isinstance(i, int)
                if not shared or i >= 2:
                    act.wait_ge(s_yd[s], 16 * nth)
                    act.wait_ge(s_dn, i - 1)
                    y_out(s)
                item_hi(i + 1, 1 - s)
                if not shared or i >= 1:
                    act.wait_ge(s_ht, i)
                    nc.scalar.copy(hT[:, 1 - s, 0], ps[:, 4, 0:256].rearrange("p (c n) -> p c n", c=2)).then_inc(s_hhi, 1)
                    act.wait_ge(s_gu, i)
                if not shared or i >= 2:
                    act.wait_ge(s_y, 2 * i)
                    act.dma_start(y_d[bass.ds((i - 2) * 128, 128), :], ysb[:, s]).then_inc(s_yd[s], 16)
                if shared:
                    if i == 0:
                        act.wait_ge(s_dready, 1)
                        down_hi(0)
                    act.wait_ge(s_gu, i + 1)
                    nc.scalar.activation(hs[:, s], ps[:, 2 + s, 0:XD], ACT.Silu).then_inc(s_silu, 1)
                    if i == 1:
                        act.wait_ge(s_ready, 2)
                        gate_up_hi(1, 0)
                        gate_up_hi(1, 1)
                    return
                nxt = act.value_load(tab[0:1, 1, bass.ds(i, 1)], min_val=0, max_val=NE)
                with act.If(nxt > 0):
                    act.wait_ge(s_dready, nxt)
                    down_hi(nxt - 1)
                with act.If(nxt % NE > 0):
                    act.wait_ge(s_ready, nxt + 1)
                    gate_up_hi(nxt, 0)
                act.wait_ge(s_gu, i + 1)
                nc.scalar.activation(hs[:, s], ps[:, 2 + s, 0:XD], ACT.Silu).then_inc(s_silu, 1)
                with act.If(nxt % NE > 0):
                    gate_up_hi(nxt, 1)

            for i in range(NT):
                step_act(i, i % 2, i // 2)
            act.wait_ge(s_tabs, 1)
            n_items = act.value_load(nit[0:1, 0:1], min_val=NT + E, max_val=MAX_ITEMS)
            with act.Fori(0, GROUPS) as group:
                with act.If(n_items > 2 * GROUP * group + NT - 1):
                    with act.Fori(0, GROUP) as pair:
                        jj = GROUP * group + pair
                        with act.If(n_items > 2 * jj + NT - 1):
                            step_act(2 * jj + NT, 0, jj + NT // 2)
                            with act.If(n_items > 2 * jj + NT):
                                step_act(2 * jj + NT + 1, 1, jj + NT // 2)
            act.wait_ge(s_yd[0], 16 * (n_items // 2) + 16)
            act.wait_ge(s_yd[1], 16 * ((n_items + 1) // 2))
            act.wait_ge(s_dn, n_items)
            y_out(0)
            act.wait_ge(s_y, 2 * n_items + 2)
            act.dma_start(y_d[bass.ds((n_items - 1) * 128, 128), :], ysb[:, 0]).then_inc(s_ylast, 16)
            act.wait_ge(s_ylast, 16)
            act.sem_inc(s_endR, 1)
            act.wait_ge(s_endR, 4)

            def diagonals(t):
                if t >= 2:
                    act.wait_ge(s_pc, t - 1)
                for k in range(K // 2):
                    nc.scalar.activation(diag[:, t % 2, k], ident[:], ACT.Copy,
                                         scale=gates[:, t, k:k + 1]).then_inc(s_dg, 1)

            diagonals(0)
            diagonals(1)
            for t in range(NT):
                act.wait_ge(s_nr, t + 1)
                nc.scalar.activation(acc[:, t % 2], acc[:, t % 2], ACT.Identity,
                                     bias=rs[:, 1:2], scale=rs[:, 0:1]).then_inc(s_hat, 1)
                if t + 2 < NT:
                    diagonals(t + 2)


        @block.vector
        def _(v):
            nv = 0
            V = nc.vector

            def step(ins):
                nonlocal nv
                ins.then_inc(s_v, 1)
                nv += 1

            def settle():
                v.wait_ge(s_v, nv)

            def split_lo(n):
                v.wait_ge(s_whi, n + 1)
                V.tensor_tensor(whl[:, n % 2, 1], wraw[:, n % 3], whl[:, n % 2, 0].bitcast(F),
                                ALU.subtract).then_inc(s_wlo, 1)

            split_lo(0)
            for t in range(NT):
                for b in range(2):
                    v.wait_ge(s_xhi, 2 * t + b + 1)
                    cols = slice(t * 128, (t + 1) * 128)
                    last = V.tensor_tensor(xT[:, 1, 4 * b:4 * b + 4, cols],
                                           ps[:, 2 * (t % 2) + b, :].rearrange("p (c n) -> p c n", c=4),
                                           xT[:, 0, 4 * b:4 * b + 4, cols].bitcast(F), ALU.subtract)
                last.then_inc(s_xlo, 1)
            v.wait_ge(s_mem, 32)
            for m in range(2):
                for b in range(2):
                    step(V.bn_stats(stat[:, m, b], memin[:, m, b * 512:(b + 1) * 512]))
            settle()
            for m in range(2):
                step(V.bn_aggr(mv[:, m], stat[:, m].rearrange("p a b -> p (a b)")))
            settle()
            V.tensor_scalar(mv[:, :, 1], mv[:, :, 1], EPS, None, ALU.add).then_inc(s_pv, 1)
            v.wait_ge(s_pw, 1)
            for m in range(2):
                V.tensor_scalar(memin[:, m], memin[:, m], mv[:, m, 0:1], mv[:, m, 1:2], ALU.subtract,
                                ALU.mult).then_inc(s_mln, 1)
            kvhi = tap = 0
            for j, w in enumerate(JOBS):
                s, b = j % 2, result(j)
                both = ps[:, b:b + 2, :].rearrange("p a n -> p (a n)")
                if w in W_JOBS and W_JOBS.index(w) < 17:
                    split_lo(W_JOBS.index(w) + 1)
                for _ in range(TAPS_IN.get(w, 0)):
                    k, c = taps[tap]
                    if k == 0:
                        v.wait_ge(s_par, 64)
                        v.wait_ge(s_const, 8)
                        if c == 0:
                            v.wait_ge(s_glu, 2)
                        step(V.tensor_scalar(cv[:, c], glu[:, c, 0:S], wdw[:, c, 0:1], cpar[:, 0, c:c + 1],
                                             ALU.mult, ALU.add))
                    else:
                        v.wait_ge(s_v, nv - 1)
                        step(V.scalar_tensor_tensor(cv[:, c], glu[:, c, k:k + S], wdw[:, c, k:k + 1], cv[:, c],
                                                    ALU.mult, ALU.add))
                    tap += 1
                if w == "a1":
                    for m in range(2):
                        v.wait_ge(s_mt, m + 1)
                        for c in range(ND):
                            step(V.tensor_scalar(mtmp[:, c, m * 128:(m + 1) * 128],
                                                 ps[:, 2 * m + c // 4, (c % 4) * 128:(c % 4 + 1) * 128],
                                                 mgb[:, 0, c:c + 1], mgb[:, 1, c:c + 1], ALU.mult, ALU.add))
                    settle()
                    v.sem_inc(s_mtc, 1)
                if w == "u1":
                    for b_ in range(2):
                        v.wait_ge(s_mhi, b_ + 1)
                        V.tensor_tensor(memT[:, 1, 4 * b_:4 * b_ + 4], mtmp[:, 4 * b_:4 * b_ + 4],
                                        memT[:, 0, 4 * b_:4 * b_ + 4].bitcast(F), ALU.subtract).then_inc(s_mlo, 1)
                if w[0] == "a":
                    c = int(w[1])
                    v.wait_ge(s_job, j + 1)
                    v.wait_ge(s_sig, c + 1)
                    V.tensor_tensor(glu[:, c, PAD:PAD + S], both, glu[:, c, PAD:PAD + S], ALU.mult).then_inc(s_glu, 1)
                    v.wait_ge(s_glu, c + 1)
                    v.sem_inc(s_gfree[s], 1)
                elif w[0] == "K":
                    kvhi += 1
                    v.wait_ge(s_kvhi, kvhi)
                    V.tensor_tensor(kT[:, 1, int(w[1])], ps[:, b, 0:M], kT[:, 0, int(w[1])].bitcast(F),
                                    ALU.subtract).then_inc(s_gfree[s], 1)
                elif w[0] == "V":
                    kvhi += 1
                    c = slice(int(w[1]) * 128, int(w[1]) * 128 + 128)
                    v.wait_ge(s_kvhi, kvhi)
                    V.tensor_tensor(vv[:, 1, :, c], ps[:, b, 0:256].rearrange("p (m n) -> p m n", m=2),
                                    vv[:, 0, :, c].bitcast(F), ALU.subtract).then_inc(s_gfree[s], 1)
                elif w == "mean":
                    v.wait_ge(s_job, j + 1)
                    for c in range(2):
                        step(V.tensor_tensor(cv[:, c], cv[:, c], both, ALU.subtract))
                    settle()
                    v.sem_inc(s_yc, 1)
                    v.sem_inc(s_gfree[s], 1)
                elif w == "var":
                    v.wait_ge(s_job, j + 1)
                    v.wait_ge(s_sd, 1)
                    step(V.reciprocal(buf2[:, 0, 0:S], buf2[:, 1, 0:S]))
                    settle()
                    for c in range(2):
                        step(V.tensor_tensor(cv[:, c], cv[:, c], buf2[:, 0, 0:S], ALU.mult))
                    settle()
                    v.sem_inc(s_yn, 1)
                if w == "q2":
                    settle()
                    v.sem_inc(s_cvd, 1)
            assert tap == len(taps)
            for n in range(4):
                v.wait_ge(s_wohi, n + 1)
                V.tensor_tensor(wo[:, 1, 2 * n:2 * n + 2], raw[:, n // 3, n % 3].rearrange("p (c n) -> p c n", c=2),
                                wo[:, 0, 2 * n:2 * n + 2].bitcast(F), ALU.subtract).then_inc(s_wolo, 1)
            v.wait_ge(s_wolo, 4)
            v.sem_inc(s_endP, 1)
            v.wait_ge(s_endP, 4)


            def q_lo(t):
                v.wait_ge(s_st, t + 1)
                V.tensor_tensor(qst[:, t % 2, 1], qT[:, :, t * 128:(t + 1) * 128],
                                qst[:, t % 2, 0].bitcast(F), ALU.subtract).then_inc(s_stl, 1)

            def row_max(t):
                v.wait_ge(s_S, t + 1)
                for hh in range(2):
                    step(V.tensor_reduce(sm[:, t % 2, 0, 2 * hh:2 * hh + 2],
                                         ps[:, 2 * (t % 2) + hh, :].rearrange("p (h n) -> p h n", h=2), AX.X, ALU.max))
                settle()
                V.tensor_scalar(sm[:, t % 2, 0], sm[:, t % 2, 0], -SCALE, None, ALU.mult).then_inc(s_negm, 1)

            q_lo(0)
            q_lo(1)
            row_max(0)
            q_lo(2)
            row_max(1)
            for t in range(NT):
                v.wait_ge(s_exp, 4 * t + 4)
                step(V.reciprocal(sm[:, t % 2, 2], sm[:, t % 2, 1]))
                settle()
                for hh in range(2):
                    heads = slice(2 * hh, 2 * hh + 2)
                    V.tensor_tensor(pr[:, t % 2, heads], pr[:, t % 2, heads],
                                    sm[:, t % 2, 2, heads].unsqueeze(2).to_broadcast([128, 2, M]),
                                    ALU.mult).then_inc(s_p, 1)
                if t + 2 < NT:
                    row_max(t + 2)
                for b in range(2):
                    v.wait_ge(s_pthi, 2 * t + b + 1)
                    cols = slice((t % 4) * 128, (t % 4 + 1) * 128)
                    V.tensor_tensor(pT[:, 1, 4 * b:4 * b + 4, cols],
                                    ps[:, 4 + b, :].rearrange("p (c n) -> p c n", c=4),
                                    pT[:, 0, 4 * b:4 * b + 4, cols].bitcast(F), ALU.subtract).then_inc(s_ptlo, 1)
                if t + 3 < NT:
                    q_lo(t + 3)

            def x1_lo(u):
                for b in range(2):
                    v.wait_ge(s_x1hi, 2 * u + b + 1)
                    V.tensor_tensor(x1T[:, 1, 4 * b:4 * b + 4],
                                    ps[:, 2 + b, :].rearrange("p (c n) -> p c n", c=4),
                                    x1T[:, 0, 4 * b:4 * b + 4].bitcast(F), ALU.subtract).then_inc(s_x1lo, 1)

            def rank(u):
                v.wait_ge(s_rk, u + 1)
                if u == NT - 1:
                    v.wait_ge(s_cnt, 1)
                step(V.tensor_tensor(ohx[:], oh[:], ps[:, rank_bank(u), 0:E].unsqueeze(1).to_broadcast([128, K, E]), ALU.mult))
                settle()
                v.sem_inc(s_rkc, 1)
                step(V.tensor_reduce(rankK[:, u], ohx[:], AX.X, ALU.add))
                settle()
                step(V.scalar_tensor_tensor(addrf[:], idxf[:, u], float(S), rankK[:, u], ALU.mult, ALU.add))
                settle()
                if u >= 2:
                    v.wait_ge(s_sc[u % 2], 16 * K * (u // 2))
                step(V.tensor_scalar(addr[:, u % 2], addrf[:], float(S), None, ALU.add))
                step(V.tensor_scalar(tok[:, u % 2:u % 2 + 1], tokf[:, 0:1], float(128 * u), None, ALU.add))
                settle()
                v.sem_inc(s_addr, 1)

            def route(u):
                v.wait_ge(s_scr, u + 1)
                step(V.tensor_tensor(sb_[:], sc[:], rbias[:], ALU.add))
                settle()
                step(V.max(top8[:], sb_[:]))
                settle()
                step(V.max_index(idxu[:], top8[:], sb_[:]))
                settle()
                step(V.tensor_copy(idxf[:, u], idxu[:]))
                settle()
                step(V.tensor_tensor(oh[:], iotaE[:].unsqueeze(1).to_broadcast([128, K, E]),
                                     idxf[:, u].unsqueeze(2).to_broadcast([128, K, E]), ALU.is_equal))
                settle()
                step(V.tensor_reduce(maskf[:], oh[:].rearrange("p k e -> p e k"), AX.X, ALU.add))
                settle()
                step(V.tensor_copy(maskb[:], maskf[:]))
                settle()
                v.sem_inc(s_mask, 1)
                step(V.tensor_tensor(ohx[:], oh[:], sc[:].unsqueeze(1).to_broadcast([128, K, E]), ALU.mult))
                step(V.tensor_tensor(cumf[:], cumf[:], maskf[:], ALU.add))
                settle()
                v.sem_inc(s_scu, 1)
                step(V.tensor_copy(cumb[:, (u + 1) % 2], cumf[:]))
                if u == NT - 1:
                    settle()
                    v.sem_inc(s_cumf, 1)
                step(V.tensor_reduce(sel[:], ohx[:], AX.X, ALU.add))
                settle()
                step(V.tensor_reduce(gs[:, 0:1], sel[:], AX.X, ALU.add))
                settle()
                step(V.reciprocal(gs[:, 1:2], gs[:, 0:1]))
                settle()
                step(V.tensor_scalar(gates[:, u], sel[:], gs[:, 1:2], ROUTED, ALU.mult, ALU.mult))

            v.wait_ge(s_wrhi, 1)
            V.tensor_tensor(wrt[:, 1], wrr[:], wrt[:, 0].bitcast(F), ALU.subtract).then_inc(s_wrl, 1)
            v.wait_ge(s_gb, 48)
            v.wait_ge(s_pt2, 8)
            for t in range(NT):
                if t >= 1:
                    x1_lo(t - 1)
                r = t % 2
                v.wait_ge(s_xr[r], 16 * (t // 2 + 1))
                for b in range(2):
                    v.wait_ge(s_pre_h if b == 0 else s_pre_pe, t + 1)
                    step(V.scalar_tensor_tensor(xres[:, r, b * 512:(b + 1) * 512],
                                                xres[:, r, b * 512:(b + 1) * 512], ALPHA, ps[:, 5 + b, :],
                                                ALU.mult, ALU.add))
                    settle()
                    v.sem_inc(s_pre, 1)
                    step(V.bn_stats(stat[:, 0, b], xres[:, r, b * 512:(b + 1) * 512]))
                settle()
                step(V.bn_aggr(mv[:, 0], stat[:, 0].rearrange("p a b -> p (a b)")))
                settle()
                V.tensor_scalar(mv[:, 0, 1:2], mv[:, 0, 1:2], EPS, None, ALU.add).then_inc(s_pv, 1)
                v.wait_ge(s_pw, 2 + t)
                V.scalar_tensor_tensor(rs[:, 1:2], mv[:, 0, 0:1], -1.0, rs[:, 0:1], ALU.mult,
                                       ALU.mult).then_inc(s_mr, 1)
                v.wait_ge(s_hat, t + 1)
                step(V.tensor_tensor(xres[:, r], xres[:, r], g1[:], ALU.mult))
                settle()
                V.tensor_tensor(xres[:, r], xres[:, r], b1[:], ALU.add).then_inc(s_x1, 1)
                if t >= 2:
                    rank(t - 2)
                if t == NT - 1:
                    x1_lo(NT - 1)
                if t >= 1:
                    route(t - 1)

            def item_tables():
                step(V.tensor_copy(cnt65[:, 1:NE], ps[:, 7, E:2 * E]))
                step(V.memset(cnt65[:, 0:1], float(S)))
                settle()
                step(V.tensor_scalar(blki[:], cnt65[:], 127.0, None, ALU.add))
                settle()
                step(V.tensor_scalar(blki[:], blki[:], 7, None, ALU.arith_shift_right))
                settle()
                step(V.tensor_copy(blk[:], blki[:]))
                settle()
                step(V.tensor_scalar(blk[:], blk[:], 1.0, None, ALU.max))
                settle()
                step(V.tensor_tensor_scan(endE[:], ones65[:], blk[:], 0.0, ALU.mult, ALU.add))
                settle()
                step(V.tensor_tensor(startE[:], endE[:], blk[:], ALU.subtract))
                for b in range(2):
                    step(V.tensor_scalar(cmp_[:, b], endE[:], itemp[:, b:b + 1], None, ALU.is_le))
                settle()
                for b in range(2):
                    step(V.tensor_tensor(cmpx[:, b], cmp_[:, b], blk[:], ALU.mult))
                settle()
                step(V.tensor_reduce(tabf[:, 0], cmp_[:], AX.X, ALU.add))
                step(V.tensor_reduce(tabf[:, 1], cmpx[:], AX.X, ALU.add))
                settle()
                step(V.tensor_tensor(tabf[:, 2], itemp[:], tabf[:, 1], ALU.subtract))
                settle()
                step(V.tensor_scalar(tabf[:, 1], tabf[:, 2], 0.0, None, ALU.is_equal))
                step(V.tensor_scalar(tabf[:, 2], tabf[:, 2], 128.0, None, ALU.mult))
                settle()
                step(V.scalar_tensor_tensor(tabf[:, 2], tabf[:, 0], float(S), tabf[:, 2], ALU.mult, ALU.add))
                step(V.tensor_scalar(cmp_[:, :, 0], tabf[:, 0], float(E), None, ALU.is_le))
                step(V.tensor_scalar(cmp_[:, :, 1], tabf[:, 0], 1.0, None, ALU.add))
                settle()
                step(V.tensor_tensor(tabf[:, 1], tabf[:, 1], cmp_[:, :, 0], ALU.mult))
                settle()
                step(V.tensor_tensor(tabf[:, 1], tabf[:, 1], cmp_[:, :, 1], ALU.mult))
                step(V.tensor_scalar(tabf[:, 0], tabf[:, 0], float(E), None, ALU.min))
                settle()
                v.sem_inc(s_cm, 1)

            def item_tables_out():
                v.wait_ge(s_tabp, 1)
                step(V.tensor_copy(tab[:].rearrange("p a b -> p (a b)"),
                                   ps[0:1, 7, 0:3 * TAB]))
                step(V.tensor_copy(nit[0:1, 0:1], endE[0:1, NE - 1:NE]))
                settle()
                v.sem_inc(s_tabs, 1)

            def lo(dst, raw_, hi, done):
                V.tensor_tensor(dst, raw_, hi.bitcast(F), ALU.subtract).then_inc(done, 1)

            def item_lo(i, s):
                for b in range(2):
                    v.wait_ge(s_ehi, 2 * i + b + 1)
                    last = V.tensor_tensor(xTe[:, s, 1, 4 * b:4 * b + 4],
                                           ps[:, b, :].rearrange("p (c n) -> p c n", c=4),
                                           xTe[:, s, 0, 4 * b:4 * b + 4].bitcast(F), ALU.subtract)
                last.then_inc(s_elo, 1)

            def gate_up_lo(e, n):
                w = bass.ds(e % 2, 1)
                v.wait_ge(s_ghi, 2 * e + n + 1)
                cols = slice(n * XD, (n + 1) * XD)
                lo(wgu[:, w, 1, :, cols].rearrange("p a c n -> p (a c) n"),
                   raw[:, w, n].rearrange("p a (c n) -> p (a c) n", c=ND),
                   wgu[:, w, 0, :, cols].rearrange("p a c n -> p (a c) n"), s_glo)

            def down_lo(e):
                w = bass.ds(e % 2, 1)
                v.wait_ge(s_dhi, e + 1)
                lo(wdn[:, w, 1].rearrange("p a c n -> p (a c) n"),
                   raw[:, w, 2].rearrange("p a (c n) -> p (a c) n", c=2),
                   wdn[:, w, 0].rearrange("p a c n -> p (a c) n"), s_dlo)

            def step_v(i, s):
                shared = isinstance(i, int)
                item_lo(i + 1, 1 - s)
                if not shared or i > 0:
                    v.wait_ge(s_hhi, i)
                    V.tensor_tensor(hT[:, 1 - s, 1], ps[:, 4, 0:256].rearrange("p (c n) -> p c n", c=2),
                                    hT[:, 1 - s, 0].bitcast(F), ALU.subtract).then_inc(s_hlo, 1)
                if shared:
                    if i == 0:
                        down_lo(0)
                else:
                    nxt = v.value_load(tab[0:1, 1, bass.ds(i, 1)], min_val=0, max_val=NE)
                    with v.If(nxt > 0):
                        down_lo(nxt - 1)
                v.wait_ge(s_silu, i + 1)
                V.tensor_tensor(hx[:, s], hs[:, s], ps[:, 2 + s, XD:2 * XD], ALU.mult).then_inc(s_h, 1)
                if not shared:
                    with v.If(nxt % NE > 0):
                        gate_up_lo(nxt, 0)
                        gate_up_lo(nxt, 1)

            def rows(t):
                step(V.tensor_tensor(oh[:], iotaE[:].unsqueeze(1).to_broadcast([128, K, E]),
                                     idxf[:, t].unsqueeze(2).to_broadcast([128, K, E]), ALU.is_equal))
                settle()
                step(V.tensor_tensor(ohx[:], oh[:], startE[:, 1:NE].unsqueeze(1).to_broadcast([128, K, E]), ALU.mult))
                settle()
                step(V.tensor_reduce(sel[:], ohx[:], AX.X, ALU.add))
                settle()
                step(V.scalar_tensor_tensor(yrow[:, t], sel[:], 128.0, rankK[:, t], ALU.mult, ALU.add))

            item_lo(0, 0)
            gate_up_lo(0, 0)
            gate_up_lo(0, 1)
            for i in range(NT):
                step_v(i, i % 2)
                if i == 0:
                    rank(NT - 2)
                    route(NT - 1)
                elif i == 1:
                    rank(NT - 1)
                elif i == 2:
                    item_tables()
                elif i == 3:
                    item_tables_out()
                    gate_up_lo(1, 0)
                    gate_up_lo(1, 1)
                else:
                    rows(2 * i - NT)
                    rows(2 * i - NT + 1)
            n_items = v.value_load(nit[0:1, 0:1], min_val=NT + E, max_val=MAX_ITEMS)
            with v.Fori(0, GROUPS) as group:
                with v.If(n_items > 2 * GROUP * group + NT - 1):
                    with v.Fori(0, GROUP) as pair:
                        jj = GROUP * group + pair
                        with v.If(n_items > 2 * jj + NT - 1):
                            step_v(2 * jj + NT, 0)
                            with v.If(n_items > 2 * jj + NT):
                                step_v(2 * jj + NT + 1, 1)
            settle()
            v.wait_ge(s_h, n_items + 1)
            v.sem_inc(s_endR, 1)
            v.wait_ge(s_endR, 4)
            for t in range(NT):
                s = t % 2
                v.wait_ge(s_cl[s], 32 * (t // 2 + 1))
                if t >= 2:
                    v.wait_ge(s_out[s], 16 * (t // 2))
                v.wait_ge(s_pc, t + 1)
                step(V.scalar_tensor_tensor(acc[:, s], x1c[:, s], ALPHA,
                                            ps[:, 2 * s:2 * s + 2, :].rearrange("p a n -> p (a n)"),
                                            ALU.mult, ALU.add))
                v.wait_ge(s_yg[s][1], 16 * (K // 2) * (t // 2 + 1))
                for k in range(K // 2, K):
                    settle()
                    step(V.scalar_tensor_tensor(acc[:, s], yg[:, s, k], gates[:, t, k:k + 1], acc[:, s],
                                                ALU.mult, ALU.add))
                settle()
                v.sem_inc(s_acc, 1)
                for b in range(2):
                    step(V.bn_stats(stat[:, 0, b], acc[:, s, b * 512:(b + 1) * 512]))
                settle()
                step(V.bn_aggr(mv[:, 0], stat[:, 0].rearrange("p a b -> p (a b)")))
                settle()
                V.tensor_scalar(mv[:, 0, 1:2], mv[:, 0, 1:2], EPS, None, ALU.add).then_inc(s_pv, 1)
                v.wait_ge(s_pw, NT + 2 + t)
                V.scalar_tensor_tensor(rs[:, 1:2], mv[:, 0, 0:1], -1.0, rs[:, 0:1], ALU.mult,
                                       ALU.mult).then_inc(s_nr, 1)
                v.wait_ge(s_hat, NT + t + 1)
                if t == 0:
                    v.wait_ge(s_g2, 32)
                step(V.tensor_tensor(acc[:, s], acc[:, s], g2[:], ALU.mult))
                settle()
                V.tensor_tensor(acc[:, s], acc[:, s], b2[:], ALU.add).then_inc(s_o, 1)

        @block.tensor
        def _(pe):
            mm = nc.tensor.matmul

            def transpose_tile(src, bank):
                for c in range(ND):
                    last = nc.tensor.transpose(ps[:, bank + c // 4, (c % 4) * 128:(c % 4 + 1) * 128],
                                               src[:, c * 128:(c + 1) * 128], ident[:])
                return last

            pe.wait_ge(s_iden, 1)
            for t in range(NT):
                pe.wait_ge(s_x[t % 3], 16 * (t // 3 + 1))
                if t >= 2:
                    pe.wait_ge(s_xlo, t - 1)
                transpose_tile(xin[:, t % 3], 2 * (t % 2)).then_inc(s_xt, 1)
            for j, w in enumerate(JOBS):
                b = result(j)
                wait_result_free(pe, j)
                if w in W_JOBS:
                    n = W_JOBS.index(w)
                    pe.wait_ge(s_wlo, n + 1)
                    wt = whl[:, n % 2]
                if w == "gate0":
                    pe.wait_ge(s_xlo, NT)
                if w == "K0":
                    pe.wait_ge(s_mlo, 2)
                if w in WCOL:
                    for h in range(2):
                        for d in range(ND):
                            for st, mo in PRODS:
                                last = mm(ps[:, b + h, :], wt[:, st, d], xT[:, mo, d, h * 512:(h + 1) * 512],
                                          start=(d == 0 and st == 0 and mo == 0), stop=(d == ND - 1 and st == 1))
                elif w[0] == "K":
                    for d in range(ND):
                        for st, mo in PRODS:
                            last = mm(ps[:, b, 0:M], wt[:, st, d], memT[:, mo, d],
                                      start=(d == 0 and st == 0 and mo == 0), stop=(d == ND - 1 and st == 1))
                elif w[0] == "V":
                    for m in range(2):
                        for d in range(ND):
                            for st, mo in PRODS:
                                last = mm(ps[:, b, m * 128:(m + 1) * 128], memT[:, st, d, m * 128:(m + 1) * 128],
                                          wt[:, mo, d], start=(d == 0 and st == 0 and mo == 0),
                                          stop=(d == ND - 1 and st == 1))
                elif w[:4] == "pool":
                    c = int(w[4])
                    pe.wait_ge(s_diff, 1)
                    pe.wait_ge(s_bd, 64)
                    for h in range(2):
                        last = mm(ps[:, b + h, :], bd[:, c], diff[:, c, h * 512:(h + 1) * 512], start=True, stop=True)
                elif w in ("mean", "var"):
                    pe.wait_ge(s_const, 8)
                    pe.wait_ge(s_cvd if w == "mean" else s_sq, 1)
                    src = cv if w == "mean" else buf1
                    for h in range(2):
                        for c in range(2):
                            last = mm(ps[:, b + h, :], ones[:], src[:, c, h * 512:(h + 1) * 512],
                                      start=(c == 0), stop=(c == 1))
                last.then_inc(s_job, 1)
                if w == "gate0":
                    for m in range(2):
                        pe.wait_ge(s_mln, m + 1)
                        transpose_tile(memin[:, m], 2 * m).then_inc(s_mt, 1)
            pe.wait_ge(s_job, len(JOBS))
            pe.sem_inc(s_endP, 1)
            pe.wait_ge(s_endP, 4)


            def scores(t):
                pe.wait_ge(s_stl, t + 1)
                if t >= 2:
                    pe.wait_ge(s_exp, 4 * (t - 1))
                for h in range(HEADS):
                    for st, mo in PRODS:
                        last = mm(ps[:, 2 * (t % 2) + h // 2, (h % 2) * M:(h % 2 + 1) * M], qst[:, t % 2, st, h],
                                  kT[:, mo, h], start=(st == 0 and mo == 0), stop=(st == 1))
                last.then_inc(s_S, 1)

            scores(0)
            scores(1)
            for t in range(NT):
                if t + 2 < NT:
                    scores(t + 2)
                for b in range(2):
                    pe.wait_ge(s_p, 2 * t + b + 1)
                    if t >= 1:
                        pe.wait_ge(s_ptlo, 2 * t - 1 + b)
                    for c in range(4):
                        h, m = 2 * b + c // 2, c % 2
                        last = nc.tensor.transpose(ps[:, 4 + b, c * 128:(c + 1) * 128],
                                                   pr[:, t % 2, h, m * 128:(m + 1) * 128], ident[:])
                    last.then_inc(s_pt, 1)
                if t % 4 == 3:
                    pe.wait_ge(s_ptlo, 2 * t + 2)
                    for h in range(HEADS):
                        n = 4 * (t // 4) + h
                        if n >= 2:
                            pe.wait_ge(s_oe, n - 1)
                        for m in range(2):
                            for st, mo in PRODS:
                                last = mm(ps[:, 6 + h % 2, :], vv[:, st, m, h * 128:(h + 1) * 128],
                                          pT[:, mo, 2 * h + m], start=(m == 0 and st == 0 and mo == 0),
                                          stop=(m == 1 and st == 1))
                        last.then_inc(s_ot, 1)

            def project(t, h):
                pe.wait_ge(s_olo, 2 * t + 2)
                if t >= 1:
                    pe.wait_ge(s_pre, 2 * t - 1 + h)
                for c in range(8):
                    for st, mo in PRODS:
                        last = mm(ps[:, 5 + h, :], mst[:, t % 2, st, c], wo[:, mo, c, h * 512:(h + 1) * 512],
                                  start=(c == 0 and st == 0 and mo == 0), stop=(c == 7 and st == 1))
                last.then_inc(s_pre_h if h == 0 else s_pre_pe, 1)

            def ranks(u):
                b = rank_bank(u)
                pe.wait_ge(s_mask, u + 1)
                if b == 7:
                    pe.wait_ge(s_scr, NT)
                if u >= 1:
                    pe.wait_ge(s_rkc, u)
                mm(ps[:, b, 0:E], tri[:], maskb[:], start=True, stop=False)
                mm(ps[:, b, 0:E], oneb[:], cumb[:, u % 2], start=False, stop=True).then_inc(s_rk, 1)

            for t in range(NT + 1):
                if t == 0:
                    pe.wait_ge(s_wrl, 1)
                    pe.wait_ge(s_wolo, 4)
                    pe.wait_ge(s_oe, 2 * HEADS)
                if t < NT:
                    project(t, 0)
                if 1 <= t <= NT:
                    pe.wait_ge(s_x1, t)
                    if t >= 2:
                        pe.wait_ge(s_x1lo, 2 * (t - 1))
                    transpose_tile(xres[:, (t - 1) % 2], 2).then_inc(s_tr, 1)
                if t < NT:
                    project(t, 1)
                if 1 <= t <= NT:
                    pe.wait_ge(s_x1lo, 2 * t)
                    if t >= 2:
                        pe.wait_ge(s_scr, t - 1)
                    for d in range(ND):
                        for st, mo in PRODS:
                            last = mm(ps[:, 7, 0:E], x1T[:, st, d], wrt[:, mo, d],
                                      start=(d == 0 and st == 0 and mo == 0), stop=(d == ND - 1 and st == 1))
                    last.then_inc(s_lg, 1)
                if 2 <= t < NT:
                    ranks(t - 2)

            def item_tables():
                pe.wait_ge(s_cm, 1)
                for f in range(3):
                    for b, n in ((0, 128), (1, TAB - 128)):
                        last = mm(ps[0:1, 7, f * TAB + b * 128:f * TAB + b * 128 + n], tabf[:, f, b:b + 1],
                                  ident[:, 0:n], start=True, stop=True)
                last.then_inc(s_tabp, 1)

            def rows_transposed(s):
                transpose_tile(xg[:, s], 0).then_inc(s_et, 1)

            pe.wait_ge(s_rkc, NT - 2)
            pe.wait_ge(s_xs[0], 16)
            rows_transposed(0)

            def gate_up(i, s, e):
                w = bass.ds(e % 2, 1)
                pe.wait_ge(s_elo, i + 1)
                pe.wait_ge(s_ghi, 2 * e + 2)
                for st, mo in ((0, 0), (1, 0), (0, 1)):
                    if mo == 1:
                        pe.wait_ge(s_glo, 2 * e + 2)
                    for d in range(ND):
                        last = mm(ps[:, 2 + s, :], xTe[:, s, st, d],
                                  wgu[:, w, mo, d].rearrange("p a n -> p (a n)"),
                                  start=(d == 0 and st == 0 and mo == 0), stop=(d == ND - 1 and mo == 1))
                last.then_inc(s_gu, 1)

            def down(i, s, e):
                w = bass.ds(e % 2, 1)
                pe.wait_ge(s_hhi, i + 1)
                pe.wait_ge(s_dhi, e + 1)
                pe.wait_ge(s_y, 2 * i + 2)
                for st, mo in ((0, 0), (1, 0), (0, 1)):
                    if st == 1:
                        pe.wait_ge(s_hlo, i + 1)
                    if mo == 1:
                        pe.wait_ge(s_dlo, e + 1)
                    for h in range(2):
                        for c in range(2):
                            last = mm(ps[:, 5 + h, :], hT[:, s, st, c],
                                      wdn[:, w, mo, c, h * 512:(h + 1) * 512].rearrange("p a n -> p (a n)"),
                                      start=(c == 0 and st == 0 and mo == 0), stop=(c == 1 and mo == 1))
                last.then_inc(s_dn, 1)

            def step_pe(i, s, nth_next):
                pe.wait_ge((s_xs if isinstance(i, int) and i + 1 < NT else s_xg)[1 - s], 16 * nth_next)
                pe.wait_ge(s_elo, i + 1)
                rows_transposed(1 - s)
                if isinstance(i, int) and i == 0:
                    gate_up(0, 0, 0)
                    return
                pe.wait_ge(s_h, i)
                if not isinstance(i, int):
                    pe.wait_ge(s_hlo, i - 1)
                for c in range(2):
                    last = nc.tensor.transpose(ps[:, 4, c * 128:(c + 1) * 128], hx[:, 1 - s, c * 128:(c + 1) * 128],
                                               ident[:])
                last.then_inc(s_ht, 1)
                e = ep = 0
                if not isinstance(i, int):
                    e = pe.value_load(tab[0:1, 0, bass.ds(i, 1)], min_val=0, max_val=E)
                    ep = pe.value_load(tab[0:1, 0, bass.ds(i - 1, 1)], min_val=0, max_val=E)
                gate_up(i, s, e)
                down(i - 1, 1 - s, ep)

            for i in range(NT):
                step_pe(i, i % 2, (i + 1) // 2 + 1 if i + 1 < NT else 1)
                if i == 0:
                    ranks(NT - 2)
                elif i == 1:
                    ranks(NT - 1)
                    pe.wait_ge(s_cumf, 1)
                    mm(ps[:, 7, E:2 * E], oneb[:], cumb[:, 0], start=True, stop=True).then_inc(s_cnt, 1)
                elif i == 3:
                    item_tables()
            pe.wait_ge(s_tabs, 1)
            n_items = pe.value_load(nit[0:1, 0:1], min_val=NT + E, max_val=MAX_ITEMS)
            with pe.Fori(0, GROUPS) as group:
                with pe.If(n_items > 2 * GROUP * group + NT - 1):
                    with pe.Fori(0, GROUP) as pair:
                        jj = GROUP * group + pair
                        with pe.If(n_items > 2 * jj + NT - 1):
                            step_pe(2 * jj + NT, 0, jj + 1)
                            with pe.If(n_items > 2 * jj + NT):
                                step_pe(2 * jj + NT + 1, 1, jj + 2)
            pe.wait_ge(s_dn, n_items)
            pe.sem_inc(s_endR, 1)
            pe.wait_ge(s_endR, 4)
            for t in range(NT):
                r = t % 2
                if t >= 2:
                    pe.wait_ge(s_acc, t - 1)
                pe.wait_ge(s_cl[r], 32 * (t // 2 + 1))
                for h in range(2):
                    mm(ps[:, 2 * r + h, :], ident[:], xsh[:, r, h * 512:(h + 1) * 512], start=True, stop=False)
                pe.wait_ge(s_dg, (K // 2) * (t + 1))
                pe.wait_ge(s_yg[r][0], 16 * (K // 2) * (t // 2 + 1))
                for k in range(K // 2):
                    for h in range(2):
                        last = mm(ps[:, 2 * r + h, :], diag[:, r, k], yg[:, r, k, h * 512:(h + 1) * 512],
                                  start=False, stop=(k == K // 2 - 1))
                last.then_inc(s_pc, 1)


def pool_edges():
    import numpy as np
    t = np.concatenate([np.arange(8), np.arange(S - 8, S)])
    e = np.zeros((128, 2, 16), np.float32)
    for g, w in enumerate(POOL_WINDOWS):
        cnt = np.minimum(t - w // 2 + w, S) - np.maximum(t - w // 2, 0)
        e[64 * (g % 2):64 * (g % 2) + 64, g // 2, :] = 1.0 / cnt
    return e


def layouts(i):
    import numpy as np
    i = {k: np.asarray(v) for k, v in i.items()}
    c = lambda x: np.ascontiguousarray(x)
    cols = lambda w: c(w.reshape(ND, 128, -1, 128).transpose(2, 1, 0, 3))
    pch = lambda v: v.reshape(-1, 128).T
    ex = lambda w, k: c(w.reshape(-1, k, 128, w.shape[-1]).transpose(0, 2, 1, 3).reshape(-1, 128, 2048))
    return {
        "x": c(i["x"].reshape(NT, 128, D)), "mem": c(i["mem"].reshape(2, 128, D)),
        "w_in": cols(i["w_in"][0]), "w_kv": cols(i["w_kv"][0]),
        "mem_gb": c(np.stack([pch(i["mem_norm_g"]), pch(i["mem_norm_b"])], 1)),
        "w_dw": c(i["w_dw"][0].T.reshape(2, 128, TAPS).transpose(1, 0, 2)),
        "cpar": c(np.stack([pch(i[k][0]) for k in ("b_dw", "conv_norm_g", "conv_norm_b", "pool_scale")], 1)),
        "edge": pool_edges(), "w_pool": c(i["w_pool"][0]),
        "w_out": c(i["w_out"][0].reshape(4, 2, 128, D).transpose(0, 2, 1, 3).reshape(4, 128, 2 * D)),
        "ln1_g": c(i["ln1_g"]), "ln1_b": c(i["ln1_b"]), "ln2_g": c(i["ln2_g"]), "ln2_b": c(i["ln2_b"]),
        "router_bias": c(i["router_bias"]),
        "w_router": c(i["w_router"][0].reshape(ND, 128, E).transpose(1, 0, 2)),
        "sh_gate": ex(i["w_gate_sh"], ND)[0], "sh_up": ex(i["w_up_sh"], ND)[0], "sh_down": ex(i["w_down_sh"], 2)[0],
        "w_gate": ex(i["w_gate"][0], ND), "w_up": ex(i["w_up"][0], ND), "w_down": ex(i["w_down"][0], 2),
    }


def kernel(**inputs):
    import numpy as np
    import concourse.bacc as bacc
    from concourse.bass_utils import run_bass_kernel_spmd

    nc = bacc.Bacc("TRN2", target_bir_lowering=False, num_devices=1)
    arrays, aps = {}, {}
    for name, v in layouts(inputs).items():
        arrays[f"in_{name}"] = v
        aps[name] = nc.dram_tensor(f"in_{name}", v.shape, mybir.dt.from_np(v.dtype), kind="ExternalInput").ap()
    out = nc.dram_tensor("out", (S, D), F, kind="ExternalOutput").ap()
    build(nc, aps, out)
    r = run_bass_kernel_spmd(nc, [arrays], core_ids=[0])
    return np.asarray(r.results[0]["out"]).reshape(1, S, D)
```
